# Optimizing a Trainium2 kernel written in Bass

```python
import jax, jax.numpy as jnp
from jax import lax
import numpy as np

D_MODEL = 2048
BATCH = 1
SEQ = 512
DEPTH = 1

MLSTM_HEADS = 4
MLSTM_DK = 256
MLSTM_DV = 256
MLSTM_CONV = 4
MLSTM_CHUNK = 64
RWKV_HEADS = 16
RWKV_HEAD = 64
RWKV_WIDTH = RWKV_HEADS * RWKV_HEAD
W_LORA = 96
A_LORA = 96
G_LORA = 256
PEER_HEADS = 8
N_KEYS = 128
N_EXPERTS = N_KEYS * N_KEYS
PEER_TOPK = 16
D_KEY = 256
EXPERT_BLOCK = 128
RMS_EPS = 1e-6
GN_EPS = 64e-5
L2_EPS = 1e-12

MLSTM_QK = MLSTM_HEADS * MLSTM_DK
MLSTM_V = MLSTM_HEADS * MLSTM_DV
MLSTM_COLS = 2 * MLSTM_QK + 2 * MLSTM_V + 2 * MLSTM_HEADS
RWKV_COLS = 3 * RWKV_WIDTH + W_LORA + A_LORA + G_LORA
GATE_COLS = 2 * D_MODEL
D_IN = MLSTM_COLS + RWKV_COLS + GATE_COLS

kernel_name = "hybrid_mlstm_rwkv7_peer_block"

def rms_norm(x, gain):
    xf = x.astype(jnp.float32)
    y = xf * lax.rsqrt(jnp.mean(xf * xf, axis=-1, keepdims=True) + RMS_EPS)
    return (y * gain.astype(jnp.float32)).astype(x.dtype)

def split_columns(p, sizes):
    offsets = np.cumsum(np.array(sizes))[:-1].tolist()
    return jnp.split(p, offsets, axis=-1)

def token_shift(p):
    return jnp.pad(p, ((0, 0), (1, 0), (0, 0)))[:, :-1]

def causal_depthwise_conv(p, w):
    K, C = w.shape
    return lax.conv_general_dilated(
        p, w[:, None, :].astype(p.dtype), window_strides=(1,), padding=[(K - 1, 0)],
        dimension_numbers=('NWC', 'WIO', 'NWC'), feature_group_count=C)

def mlstm_chunkwise(q, k, v, ig, lf):
    B, H, T, DK = q.shape
    DV = v.shape[-1]
    L = MLSTM_CHUNK
    NC = T // L
    q = q * DK ** -0.5
    causal = jnp.tril(jnp.ones((L, L), dtype=bool))

    def chunks(t):
        return jnp.moveaxis(t.reshape(B, H, NC, L, *t.shape[3:]), 2, 0)

    def step(carry, xs):
        C, n, m = carry
        qc, kc, vc, igc, lfc = xs
        b = jnp.cumsum(lfc, axis=-1)
        dmat = b[..., :, None] - b[..., None, :] + igc[..., None, :]
        dmat = jnp.where(causal, dmat, -jnp.inf)
        inter = b + m[..., None]
        m_t = jnp.maximum(inter, jnp.max(dmat, axis=-1))
        s = jnp.einsum('bhtd,bhsd->bhts', qc, kc) * jnp.exp(dmat - m_t[..., None])
        w_inter = jnp.exp(inter - m_t)
        num = (jnp.einsum('bhts,bhsv->bhtv', s, vc)
               + w_inter[..., None] * jnp.einsum('bhtd,bhdv->bhtv', qc, C))
        den = jnp.sum(s, axis=-1) + w_inter * jnp.einsum('bhtd,bhd->bht', qc, n)
        h = num / jnp.maximum(jnp.abs(den), jnp.exp(-m_t))[..., None]
        g_end = b[..., -1:] - b + igc
        m_new = jnp.maximum(b[..., -1] + m, jnp.max(g_end, axis=-1))
        decay = jnp.exp(b[..., -1] + m - m_new)
        ws = jnp.exp(g_end - m_new[..., None])
        C_new = decay[..., None, None] * C + jnp.einsum('bhsd,bhsv->bhdv', kc * ws[..., None], vc)
        n_new = decay[..., None] * n + jnp.einsum('bhsd,bhs->bhd', kc, ws)
        return (C_new, n_new, m_new), h

    init = (jnp.zeros((B, H, DK, DV), jnp.float32),
            jnp.zeros((B, H, DK), jnp.float32),
            jnp.zeros((B, H), jnp.float32))
    _, h = lax.scan(step, init, tuple(chunks(t) for t in (q, k, v, ig, lf)))
    return jnp.moveaxis(h, 0, 2).reshape(B, H, T, DV)

def mlstm_branch(p, conv_w, b_i, b_f):
    B, T, _ = p.shape
    qk, v, o, i_pre, f_pre = split_columns(p, (2 * MLSTM_QK, MLSTM_V, MLSTM_V, MLSTM_HEADS, MLSTM_HEADS))
    qk = jax.nn.silu(causal_depthwise_conv(qk, conv_w))
    q, k = jnp.split(qk, 2, axis=-1)

    def heads(t):
        return t.reshape(B, T, MLSTM_HEADS, -1).transpose(0, 2, 1, 3).astype(jnp.float32)

    ig = (i_pre + b_i).astype(jnp.float32).transpose(0, 2, 1)
    lf = jax.nn.log_sigmoid((f_pre + b_f).astype(jnp.float32)).transpose(0, 2, 1)
    h = mlstm_chunkwise(heads(q), heads(k), heads(v), ig, lf)
    h = h.transpose(0, 2, 1, 3).reshape(B, T, MLSTM_V).astype(p.dtype)
    return jax.nn.sigmoid(o) * h

def wkv7_scan(r, decay, k, v, aa, bb):
    B, T, H, N = r.shape
    xs = tuple(jnp.moveaxis(t, 1, 0) for t in (r, decay, k, v, aa, bb))

    def step(S, inp):
        r_t, w_t, k_t, v_t, a_t, b_t = inp
        sa = jnp.einsum('bhvk,bhk->bhv', S, a_t)
        S = (S * w_t[:, :, None, :] + sa[..., None] * b_t[:, :, None, :]
             + v_t[..., None] * k_t[:, :, None, :])
        return S, jnp.einsum('bhvk,bhk->bhv', S, r_t)

    _, y = lax.scan(step, jnp.zeros((B, H, N, N), jnp.float32), xs)
    return jnp.moveaxis(y, 0, 1)

def rwkv7_branch(p, mu, w0, w2, a0, a2, g2, k_k, k_a, r_k, ln_w, ln_b):
    B, T, _ = p.shape
    p = p + (token_shift(p) - p) * mu
    r, k, v, wl, al, gl = split_columns(p, (RWKV_WIDTH, RWKV_WIDTH, RWKV_WIDTH, W_LORA, A_LORA, G_LORA))
    w = -jax.nn.softplus(-(w0 + jnp.tanh(wl) @ w2).astype(jnp.float32)) - 0.5
    decay = jnp.exp(-jnp.exp(w))
    a = jax.nn.sigmoid((a0 + al @ a2).astype(jnp.float32))
    g = jax.nn.sigmoid(gl) @ g2

    def heads(t):
        return t.astype(jnp.float32).reshape(B, T, RWKV_HEADS, RWKV_HEAD)

    kk = heads(k * k_k)
    kk = kk / jnp.maximum(jnp.sqrt(jnp.sum(kk * kk, axis=-1, keepdims=True)), L2_EPS)
    k = k.astype(jnp.float32) * (1.0 + (a - 1.0) * k_a)
    rh, kh, vh = heads(r), heads(k), heads(v)
    y = wkv7_scan(rh, heads(decay), kh, vh, -kk, kk * heads(a))
    mean = jnp.mean(y, axis=-1, keepdims=True)
    var = jnp.mean(jnp.square(y - mean), axis=-1, keepdims=True)
    y = ((y - mean) * lax.rsqrt(var + GN_EPS)).reshape(B, T, RWKV_WIDTH)
    y = y * ln_w.astype(jnp.float32) + ln_b.astype(jnp.float32)
    bonus = jnp.sum(rh * kh * r_k.astype(jnp.float32), axis=-1, keepdims=True) * vh
    y = y + bonus.reshape(B, T, RWKV_WIDTH)
    return y.astype(p.dtype) * g

def peer_ffn(xn, w_query, sub_keys, expert_u, expert_v):
    B, T, D = xn.shape
    NT = B * T
    xt = xn.reshape(NT, D)
    q = (xt @ w_query).reshape(NT, PEER_HEADS, 2, D_KEY // 2).astype(jnp.float32)
    s = jnp.einsum('nhpd,pkd->nhpk', q, sub_keys.astype(jnp.float32))
    v1, i1 = lax.top_k(s[:, :, 0], PEER_TOPK)
    v2, i2 = lax.top_k(s[:, :, 1], PEER_TOPK)
    cand = (v1[..., :, None] + v2[..., None, :]).reshape(NT, PEER_HEADS, PEER_TOPK * PEER_TOPK)
    best, ci = lax.top_k(cand, PEER_TOPK)
    e1 = jnp.take_along_axis(i1, ci // PEER_TOPK, axis=-1)
    e2 = jnp.take_along_axis(i2, ci % PEER_TOPK, axis=-1)
    idx = e1 * N_KEYS + e2
    gate = jax.nn.softmax(best, axis=-1)
    NB = NT // EXPERT_BLOCK
    HK = PEER_HEADS * PEER_TOPK
    xb = xt.reshape(NB, EXPERT_BLOCK, D)
    ib = idx.reshape(NB, EXPERT_BLOCK, HK)
    gb = gate.reshape(NB, EXPERT_BLOCK, HK)

    def block(args):
        xc, ic, gc = args
        act = jax.nn.gelu(jnp.einsum('cd,ced->ce', xc, expert_u[ic]), approximate=False)
        return jnp.einsum('ce,ced->cd', (gc * act).astype(xc.dtype), expert_v[ic])

    return lax.map(block, (xb, ib, gb)).reshape(B, T, D)

def setup_inputs(seed: int = 0) -> dict:
    key = jax.random.key(seed)
    ks = jax.random.split(key, 32)
    L = DEPTH

    def nrm(k, shape, scale):
        return jax.random.normal(k, shape, jnp.float32) * scale

    return {
        "x": nrm(ks[0], (BATCH, SEQ, D_MODEL), 1.0),
        "norm_mix_gain": 1.0 + nrm(ks[1], (L, D_MODEL), 0.05),
        "w_in": nrm(ks[2], (L, D_MODEL, D_IN), D_MODEL ** -0.5),
        "mlstm_conv": nrm(ks[3], (L, MLSTM_CONV, 2 * MLSTM_QK), MLSTM_CONV ** -0.5),
        "mlstm_b_i": nrm(ks[4], (L, MLSTM_HEADS), 0.1),
        "mlstm_b_f": jnp.linspace(3.0, 6.0, MLSTM_HEADS, dtype=jnp.float32)[None] + nrm(ks[5], (L, MLSTM_HEADS), 0.1),
        "rwkv_mu": jax.random.uniform(ks[6], (L, RWKV_COLS), jnp.float32),
        "rwkv_w0": nrm(ks[7], (L, RWKV_WIDTH), 0.5),
        "rwkv_w2": nrm(ks[8], (L, W_LORA, RWKV_WIDTH), W_LORA ** -0.5),
        "rwkv_a0": nrm(ks[9], (L, RWKV_WIDTH), 0.1),
        "rwkv_a2": nrm(ks[10], (L, A_LORA, RWKV_WIDTH), A_LORA ** -0.5),
        "rwkv_g2": nrm(ks[11], (L, G_LORA, RWKV_WIDTH), G_LORA ** -0.5),
        "rwkv_k_k": 0.85 + nrm(ks[12], (L, RWKV_WIDTH), 0.1),
        "rwkv_k_a": 1.0 + nrm(ks[13], (L, RWKV_WIDTH), 0.1),
        "rwkv_r_k": nrm(ks[14], (L, RWKV_HEADS, RWKV_HEAD), 0.1),
        "rwkv_ln_w": 1.0 + nrm(ks[15], (L, RWKV_WIDTH), 0.05),
        "rwkv_ln_b": nrm(ks[16], (L, RWKV_WIDTH), 0.01),
        "proj_mlstm": nrm(ks[17], (L, MLSTM_V, D_MODEL), MLSTM_V ** -0.5),
        "proj_rwkv": nrm(ks[18], (L, RWKV_WIDTH, D_MODEL), RWKV_WIDTH ** -0.5),
        "w_out": nrm(ks[19], (L, D_MODEL, D_MODEL), D_MODEL ** -0.5),
        "norm_ffn_gain": 1.0 + nrm(ks[20], (L, D_MODEL), 0.05),
        "peer_w_query": nrm(ks[21], (L, D_MODEL, PEER_HEADS * D_KEY), D_MODEL ** -0.5),
        "peer_sub_keys": nrm(ks[22], (L, 2, N_KEYS, D_KEY // 2), (D_KEY // 2) ** -0.5),
        "peer_u": nrm(ks[23], (L, N_EXPERTS, D_MODEL), D_MODEL ** -0.5),
        "peer_v": nrm(ks[24], (L, N_EXPERTS, D_MODEL), 0.5 * PEER_HEADS ** -0.5),
        "norm_final_gain": 1.0 + nrm(ks[25], (D_MODEL,), 0.05),
    }

def reference(x, norm_mix_gain, w_in, mlstm_conv, mlstm_b_i, mlstm_b_f, rwkv_mu, rwkv_w0, rwkv_w2,
              rwkv_a0, rwkv_a2, rwkv_g2, rwkv_k_k, rwkv_k_a, rwkv_r_k, rwkv_ln_w, rwkv_ln_b,
              proj_mlstm, proj_rwkv, w_out, norm_ffn_gain, peer_w_query, peer_sub_keys,
              peer_u, peer_v, norm_final_gain):
    h = x
    for l in range(DEPTH):
        xn = rms_norm(h, norm_mix_gain[l])
        p = xn @ w_in[l]
        p_m, p_r, p_g = split_columns(p, (MLSTM_COLS, RWKV_COLS, GATE_COLS))
        y_m = mlstm_branch(p_m, mlstm_conv[l], mlstm_b_i[l], mlstm_b_f[l])
        y_r = rwkv7_branch(p_r, rwkv_mu[l], rwkv_w0[l], rwkv_w2[l], rwkv_a0[l], rwkv_a2[l],
                           rwkv_g2[l], rwkv_k_k[l], rwkv_k_a[l], rwkv_r_k[l], rwkv_ln_w[l], rwkv_ln_b[l])
        g_m, g_r = jnp.split(jax.nn.sigmoid(p_g), 2, axis=-1)
        mixed = g_m * (y_m @ proj_mlstm[l]) + g_r * (y_r @ proj_rwkv[l])
        h = h + mixed @ w_out[l]
        h = h + peer_ffn(rms_norm(h, norm_ffn_gain[l]), peer_w_query[l], peer_sub_keys[l],
                         peer_u[l], peer_v[l])
    return rms_norm(h, norm_final_gain)


_drawn_inputs = setup_inputs


def setup_inputs(seed=0):
    import zlib

    import numpy as np

    out = dict(_drawn_inputs(seed))
    spreads = {}
    factors = {'mlstm_b_i': 8.0,
     'rwkv_a0': 3.249,
     'rwkv_k_k': 5.373,
     'rwkv_ln_w': 3.296,
     'rwkv_ln_b': 8.0,
     'norm_ffn_gain': 2.74}
    for name, (base, spread) in spreads.items():
        noise = np.random.default_rng([zlib.crc32(name.encode()), seed]).standard_normal(out[name].shape)
        drawn = base * np.exp(spread * noise) if base else spread * noise
        out[name] = __import__('jax').numpy.asarray(drawn.astype(out[name].dtype))
    for name, factor in factors.items():
        out[name] = (out[name] * factor).astype(out[name].dtype)
    return out
```

```python
from contextlib import ExitStack

import concourse.bass as bass
from concourse import mybir
from concourse.alu_op_type import AluOpType as ALU

F32 = mybir.dt.float32
F32R = mybir.dt.float32r
BF16 = mybir.dt.bfloat16
U32 = mybir.dt.uint32
ACT = mybir.ActivationFunctionType
AX = mybir.AxisListType

P = 128
T = 512
TT = T // P
D = 2048
KT = D // P
CH = 64
NCH = T // CH
RJ = 1024 // P
MH = 4
HEADS, TOPK, NKEYS = 8, 16, 128
DECAY = float(2.718281828459045 ** -0.5)
RMS_EPS, GN_EPS, L2_EPS = 1e-6, 64e-5, 1e-12
LEVELS = [1, 2, 4, 8, 16, 32]

N_LORA = 4
N_SIDE = 4
U_RWKV = N_LORA
U_MLSTM = U_RWKV + (4 + N_SIDE) * RJ
U_MIX = U_MLSTM + 6 * MH
U_OUT = U_MIX + KT
U_QUERY = U_OUT + KT
GROUPS = NKEYS // 2
AHEAD = HEADS + 2
U_TAIL = U_QUERY + 4 * HEADS
U_PEER = U_TAIL + 2 * (AHEAD - HEADS)
U_SCORED = U_PEER + 2 * (AHEAD - 1)
N_UNITS = U_PEER + 2 * GROUPS + 2 * (GROUPS - AHEAD)

F_TR, F_INTRA, F_X0, F_LEVEL, F_W, F_G, F_U, F_S = 2, 2, 2, 4, 2, 2, 3, 2

C_RP, N_RP = 0, 10
C_LMU = C_RP + RJ * N_RP
C_BI = C_LMU + N_LORA
C_CONV = C_BI + 2
C_GAIN = C_CONV + 16 * 4
N_PAR = C_GAIN + 3 * KT


class Steps:

    def __init__(self, eng, sem):
        self.eng, self.sem, self.base, self.n = eng, sem, 0, 0

    def __call__(self, ins):
        ins.then_inc(self.sem, 1)
        self.n += 1
        self.eng.wait_ge(self.sem, self.base + self.n)

    def enter(self, i, first, per):
        self.kept = (self.base, self.n, per)
        self.base, self.n = per * (i - first) + (self.base + self.n), 0

    def leave(self, times):
        base, n, per = self.kept
        assert self.n == per, f"steps in the loop's body: {self.n}"
        self.base, self.n = base, n + per * times


def own(eng, ins, sem, value):
    ins.then_inc(sem, 1)
    eng.wait_ge(sem, value)


def build(nc, stream, lora_w, params, x_t, keys_t, out_t):
    dram = lambda name, shape: nc.dram_tensor(name, shape, F32, kind="Internal").ap()
    yr_d = dram("yr_scratch", (RJ, P, T))
    ym_d = dram("ym_scratch", (2 * MH, P, T))
    og_d = dram("ogate_scratch", (2 * MH, P, T))
    if_d = dram("if_scratch", (2, MH, T))
    sg_d = dram("mergegate_scratch", (2 * KT, P, T))
    act_d = dram("gelu_scratch", (2 * AHEAD, P, T))
    GB = 16
    GT = T // GB
    gate_d = dram("gates_scratch", (GB, P, NKEYS, GT))

    ctx = ExitStack()
    with ctx:
        stack = [ctx]
        sb = lambda name, shape, dt=F32: stack[-1].enter_context(nc.sbuf_tensor(name, shape, dt))
        sem = lambda name: ctx.enter_context(nc.semaphore(name))
        ps = ctx.enter_context(nc.psum_tensor("ps", [P, 8, 512], F32))
        bank = lambda b: ps[:, b, :]

        xh = sb("xh", [P, KT, T], F32R)
        xl = sb("xl", [P, KT, T], F32R)
        raw = [sb(f"raw{s}", [P, 2048]) for s in range(2)]
        wh = [sb(f"wh{s}", [P, 2048], F32R) for s in range(2)]
        wl = [sb(f"wl{s}", [P, 2048], F32R) for s in range(2)]
        par = sb("par", [P, N_PAR])
        ident = sb("ident", [P, P])
        ones = sb("ones", [P, P])
        headones = sb("headones", [P, P])
        tri = sb("tri", [P, P], BF16)
        cst = sb("cst", [P, 4])
        iota16 = sb("iota16", [P, TOPK]); iota128 = sb("iota128", [P, P])

        def phase():
            if len(stack) > 1:
                stack.pop().close()
            stack.append(ExitStack())

        phase()
        H1 = sb("h_in", [P, KT, T])
        sq1 = sb("sq1", [P, 2, T]); nt1 = sb("nt1", [P, 2, T]); rstd1 = sb("rstd1", [P, T])
        phase()
        lora = sb("lora", [P, N_LORA, T])
        lw = sb("lw", [P, N_LORA, P])
        pin = [sb(f"pin{c}", [P, T + 1]) for c in range(3)]
        plo = pin[0]
        g_sb = sb("g_sb", [P, T]); bonus = sb("bonus", [P, T])
        AR = sb("AR", [P, 2, T]); Bt = sb("Bt", [P, T]); Kt = sb("Kt", [P, T])
        Vn = sb("Vn", [P, TT, P]); Bn = sb("Bn", [P, TT, P]); Kn = sb("Kn", [P, TT, P]); An = sb("An", [P, TT, P])
        WT = sb("WT", [P, T]); Gn = sb("Gn", [P, 2, TT, CH]); Un = sb("Un", [P, TT, 2, CH])
        Sh = sb("Sh", [P, NCH + 1, P]); SE = sb("SE", [P, P]); EL = sb("EL", [P, NCH])
        ysb = sb("ysb", [P, T]); yc = sb("yc", [P, T]); ysq = sb("ysq", [P, T])
        sgb = sb("sgb", [P, 2, T])
        mask4 = sb("mask4", [P, 4, P], BF16)
        lev = sb("lev", [P, len(LEVELS), P], BF16)
        reset = sb("reset", [P, T], BF16)
        over = sb("over", [P, 16, T])
        r_, k_, v_, sg, cs, E0, E1, E2, a_, kk, t1, t2 = (over[:, n, :] for n in range(12))
        M4 = over[:, 0:8, :].rearrange("p n (a t) -> p n a t", a=4)
        X = over[:, 8:10, :].rearrange("p n (a t) -> p (n a) t", a=4)
        XT = over[:, 10:12, :].rearrange("p n (a t) -> p (n a) t", a=4)
        Z = over[:, 12:14, :].rearrange("p n (a t) -> p (n a) t", a=4)
        Mb = over[:, 14:16, :].rearrange("p n (a t) -> p (n a) t", a=4)
        AKVf = over[:, 12:14, :].rearrange("p n t -> p (n t)")
        AKV = AKVf[:, 0:T].rearrange("p (h n c) -> p h n c", h=2, n=TT)
        phase()
        rows = sb("rows", [MH, 8, T])
        rcol = sb("rcol", [P, TT, MH])
        RNb = sb("RNb", [P, MH, 2, T])
        pc = [sb(f"pc{c}", [P, T + 3]) for c in range(4)]
        cacc = sb("cacc", [P, 2, T])
        QK = sb("QK", [P, 4, T])
        Vm = sb("Vm", [P, TT, 256])
        Dm = sb("Dm", [P, TT, T]); SD = sb("SD", [P, TT, T])
        sel = sb("sel", [MH, MH, P])
        og = sb("og", [P, 2, T]); rec = sb("rec", [P, T]); hv = sb("hv", [P, 2, T]); ymo = sb("ymo", [P, 2, T])
        phase()
        yh = sb("yh", [P, 16, T], F32R); yl = sb("yl", [P, 16, T], F32R)
        yraw = sb("yraw", [P, 4, T])
        sgm = sb("sgm", [P, 2, 2, T]); mxo = sb("mxo", [P, 2, T])
        phase()
        H = sb("H", [P, KT, T])

        def subphase():
            stack.pop().close()
            stack.append(ExitStack())

        stack.append(ExitStack())
        sq2 = sb("sq2", [P, 2, T]); nt2 = sb("nt2", [P, 2, T]); rstd2 = sb("rstd2", [P, T])
        subphase()
        EGT = sb("EGT", [P, 3, T])
        stack.append(ExitStack())
        EG = sb("EG", [P, 3, TT, P])
        keys = sb("keys", [P, 2, P])
        qsb = sb("qsb", [P, 2, T]); preb = sb("preb", [P, 2, T])
        ssb = sb("ssb", [P, 2, TT, P]); srep = sb("srep", [P, P])
        v16 = sb("v16", [P, 2, TT, TOPK]); i16 = sb("i16", [P, 2, TT, TOPK], U32); if16 = sb("if16", [P, 2, TT, TOPK])
        cand = sb("cand", [P, 256]); crep = sb("crep", [P, 256])
        best = sb("best", [P, TT, TOPK]); ci = sb("ci", [P, TT, TOPK], U32)
        chi = sb("chi", [P, 2, TT, TOPK], U32); chf = sb("chf", [P, 2, TT, TOPK])
        eq = sb("eq", [P, TOPK, TOPK])
        ex = sb("ex", [P, TT, TOPK]); sm = sb("sm", [P, 2, TT])
        subphase()
        OH = 8
        oh = [[sb(f"oh{s}{c}", [P, P]) for c in range(2)] for s in range(OH)]
        stage = [sb(f"stage{s}", [P, NKEYS, GT]) for s in range(2)]
        stack.pop().close()
        subphase()
        gt = sb("gt", [P, 2, T]); act_ = sb("act_", [P, 2, T])
        gah = [sb(f"gah{s}", [P, 2, T], F32R) for s in range(2)]
        gal = [sb(f"gal{s}", [P, 2, T], F32R) for s in range(2)]
        sq3 = sb("sq3", [P, 2, T]); rstd3 = sb("rstd3", [P, T])
        stack.pop().close()
        stack.pop().close()

        w_loaded = [sem("w_loaded0"), sem("w_loaded1")]
        w_hi, w_lo, w_used = sem("w_hi"), sem("w_lo"), sem("w_used")
        par_in, x_in, keys_in = sem("par_in"), [sem(f"x_in{c}") for c in range(4)], sem("keys_in")
        consts = sem("consts")
        passed = sem("passed")
        pool_step, dve_step, act_step = sem("pool_step"), sem("dve_step"), sem("act_step")
        sq_ready, sq_used = sem("sq_ready"), sem("sq_used")
        var_ready, std_ready, nt_ready, nh_ready, nl_ready = (sem(n) for n in ("var_ready", "std_ready", "nt_ready", "nh_ready", "nl_ready"))
        lora_p, lora_s, lora_ready = sem("lora_p"), sem("lora_s"), sem("lora_ready")
        lw_in, lw_mm, lw_taken = sem("lw_in"), sem("lw_mm"), sem("lw_taken")
        pin_saved, shifted = sem("pin_saved"), sem("shifted")
        cs_ready, exps_ready, kk_ready, kksum_ready, kknorm_ready = (sem(n) for n in ("cs_ready", "exps_ready", "kk_ready", "kksum_ready", "kknorm_ready"))
        bprod_ready, bsum_ready, prep_done = sem("bprod_ready"), sem("bsum_ready"), sem("prep_done")
        tr_ready, tr_savedA, tr_savedD = sem("tr_ready"), sem("tr_savedA"), sem("tr_savedD")
        intra_ready, intra_saved = sem("intra_ready"), sem("intra_saved")
        xt0_ready, x0_ready, x0_saved, mb_ready = sem("xt0_ready"), sem("x0_ready"), sem("x0_saved"), sem("mb_ready")
        z_ready, z_saved, xx_ready, xt_ready = sem("z_ready"), sem("z_saved"), sem("xx_ready"), sem("xt_ready")
        x_saved, xt_saved = sem("x_saved"), sem("xt_saved")
        wt_ready, wt_saved, akv_ready, akv_saved, g_ready, g_saved = (sem(n) for n in ("wt_ready", "wt_saved", "akv_ready", "akv_saved", "g_ready", "g_saved"))
        u_ready, u_saved, s_ready, s_saved = sem("u_ready"), sem("u_saved"), sem("s_ready"), sem("s_saved")
        y_ready, y_saved, mean_ready, ysq_ready, yvar_ready, ystd_ready, yo_ready = (sem(n) for n in ("y_ready", "y_saved", "mean_ready", "ysq_ready", "yvar_ready", "ystd_ready", "yo_ready"))
        side_saved, yr_stored, if_stored = sem("side_saved"), sem("yr_stored"), sem("if_stored")
        sg_stored = [sem("sg_stored0"), sem("sg_stored1")]
        rows_in, rows_ready, rc_ready, rb_ready, rb_saved = sem("rows_in"), sem("rows_ready"), sem("rc_ready"), sem("rb_ready"), sem("rb_saved")
        lf_e, lf_ln, nm_ready = sem("lf_e"), sem("lf_ln"), sem("nm_ready")
        pc_saved, conv_ready, qk_ready, v_saved = sem("pc_saved"), sem("conv_ready"), sem("qk_ready"), sem("v_saved")
        arg_ready, dm_ready, sc_ready, sd_ready = sem("arg_ready"), sem("dm_ready"), sem("sc_ready"), sem("sd_ready")
        hm_ready, ym_ready, ym_stored, og_in, og_used = sem("hm_ready"), sem("ym_ready"), sem("ym_stored"), sem("og_in"), sem("og_used")
        yraw_in, yh_ready, yl_ready = sem("yraw_in"), sem("yh_ready"), sem("yl_ready")
        sg_in, mix_ready = [sem("sg_in0"), sem("sg_in1")], sem("mix_ready")
        mh_ready, ml_ready, h_in, h_ready = sem("mh_ready"), sem("ml_ready"), sem("h_in"), sem("h_ready")
        pre_ready, pre_in = sem("pre_ready"), sem("pre_in")
        pre_stored = [sem("pre_stored0"), sem("pre_stored1")]
        q_saved, key_scores, ssb_saved, sel_done = sem("q_saved"), sem("key_scores"), sem("ssb_saved"), sem("sel_done")
        best_ready, ex_ready, routed, egt_ready, egt_saved = sem("best_ready"), sem("ex_ready"), sem("routed"), sem("egt_ready"), sem("egt_saved")
        oh_ready, dense_saved, oh_used = sem("oh_ready"), sem("dense_saved"), sem("oh_used")
        gates_stored = [sem("gates_stored0"), sem("gates_stored1")]
        gt_in, gelu_ready, ga_ready, gah_ready, gal_ready = sem("gt_in"), sem("gelu_ready"), sem("ga_ready"), sem("gah_ready"), sem("gal_ready")
        out_ready, out_added, last_ready, out_stored = sem("out_ready"), sem("out_added"), sem("last_ready"), sem("out_stored")

        rp = lambda j, c: par[:, bass.ds(j * N_RP + c, 1)]

        def load_unit(sp, n, s, first=False):
            if not first:
                sp.wait_ge(w_lo, n - 1)
            sp.dma_start(raw[s][:, :], stream[bass.ds(n, 1)].rearrange("a p n -> p (a n)")).then_inc(w_loaded[s], 16)

        def split_hi(act, n, s, first=False):
            act.wait_ge(w_loaded[s], 8 * n + 16 - 8 * s)
            if not first:
                act.wait_ge(w_used, n - 1)
            act.activation(wh[s][:, :], raw[s][:, :], ACT.Copy).then_inc(w_hi, 1)

        def split_lo(pool, n, s):
            pool.wait_ge(w_hi, n + 1)
            pool.tensor_tensor(wl[s][:, :], raw[s][:, :], wh[s][:, :].bitcast(F32), ALU.subtract).then_inc(w_lo, 1)

        def products(pe, dst, s, k, n, h, l, kx, start, stop):
            w_h, w_l = wh[s][:, k * P:(k + 1) * P], wl[s][:, k * P:(k + 1) * P]
            pe.matmul(dst, w_h, h[:, kx, :], start=start, stop=False)
            pe.matmul(dst, w_h, l[:, kx, :], start=False, stop=False)
            return pe.matmul(dst, w_l, h[:, kx, :], start=False, stop=stop)

        def unit(pe, n, s, dst, k0=0, k1=KT):
            if k0 == 0:
                pe.wait_ge(w_lo, n + 1)
            for k in range(k0, k1):
                last = products(pe, dst, s, k, P, xh, xl, k, k == 0, k == KT - 1)
            if k1 == KT:
                last.then_inc(w_used, 1)

        class Filler:
            def __init__(self, pe, n, units, waits):
                self.pe, self.n, self.units, self.at, self.waits = pe, n, units, 0, waits

            def __call__(self, m):
                for _ in range(m):
                    c, k = divmod(self.at, KT)
                    if c < self.units:
                        if k == 0:
                            self.waits(c)
                        unit(self.pe, self.n + c, c % 2, bank(6 + c % 2), k, k + 1)
                        self.at += 1

        class Follower:
            def __init__(self, units, keep):
                self.units, self.at, self.keep = units, 0, keep

            def __call__(self, m):
                for _ in range(m):
                    self.at += 1
                    if self.at % KT == 0 and self.at // KT <= self.units:
                        self.keep(self.at // KT - 1)

        def tile_unit(i, c):
            return U_RWKV + c if isinstance(i, int) and i == 0 else U_RWKV + 8 * i - 4 + c

        block = ctx.enter_context(nc.Block())

        @block.sync
        def _(sp):
            sp.dma_start(par[:, :], params).then_inc(par_in, 16)
            for c in range(4):
                sp.dma_start(H1[:, 4 * c:4 * c + 4, :], x_t[4 * c:4 * c + 4].rearrange("k p t -> p k t")).then_inc(x_in[c], 16)
            for n in range(2):
                load_unit(sp, n, n, first=True)
            for n in range(2, N_LORA):
                load_unit(sp, n, n % 2)
            sp.wait_ge(nl_ready, KT)
            def load_lora(j):
                sp.dma_start(lw[:, :, :], lora_w[bass.ds(j, 1)].rearrange("a p c n -> p (a c) n")).then_inc(lw_in, 16)

            for c in range(4):
                load_unit(sp, U_RWKV + c, c % 2)
            load_lora(0)
            with sp.Fori(1, RJ) as j:
                for c in range(4 + N_SIDE):
                    load_unit(sp, tile_unit(j, c), c % 2)
                sp.wait_ge(lw_mm, 3 * j)
                load_lora(j)
            for c in range(N_SIDE):
                load_unit(sp, U_MLSTM - N_SIDE + c, c % 2)
            for c in range(2):
                load_unit(sp, U_MLSTM + c, c)
            sp.wait_ge(if_stored, 32)
            sp.wait_ge(yr_stored, 16 * RJ)
            for c in range(2):
                sp.dma_start(rows[:, c, :], if_d[c]).then_inc(rows_in, 16)
            for s, stores in enumerate((2 * RJ, 3 * RJ)):
                sp.wait_ge(sg_stored[s], 16 * (stores + 1))
            for c in range(2, 6):
                load_unit(sp, U_MLSTM + c, c % 2)
            with sp.Fori(1, MH) as h:
                for c in range(6):
                    load_unit(sp, U_MLSTM + 6 * h + c, c % 2)
            def load_merge(d, dd):
                for c in range(2):
                    sp.dma_start(sgm[:, dd, c, :], sg_d[bass.ds(2 * d + dd + KT * c, 1)].rearrange("a p t -> p (a t)")).then_inc(sg_in[dd], 16)

            for dd in range(2):
                load_unit(sp, U_MIX + dd, dd)
            sp.wait_ge(ym_stored, 16 * MH)
            for dd in range(2):
                load_merge(0, dd)
            with sp.Fori(1, KT // 2) as d:
                for dd in range(2):
                    load_unit(sp, U_MIX + 2 * d + dd, dd)
                    sp.wait_ge(mix_ready, 2 * d + dd - 1)
                    load_merge(d, dd)
            with sp.Fori(0, KT // 2) as d:
                for c in range(2):
                    load_unit(sp, U_OUT + 2 * d + c, c)
            with sp.Fori(0, 2 * HEADS) as h:
                for c in range(2):
                    load_unit(sp, U_QUERY + 2 * h + c, c)
            with sp.Fori(0, (N_UNITS - U_TAIL) // 2) as g:
                for c in range(2):
                    load_unit(sp, U_TAIL + 2 * g + c, c)
            for k in range(KT):
                sp.wait_ge(last_ready, k + 1)
                sp.dma_start(out_t[k], H[:, k, :]).then_inc(out_stored, 16)
            sp.wait_ge(out_stored, 16 * KT)

        @block.gpsimd
        def _(pool):
            step = Steps(pool, pool_step)
            sel_ge = lambda v, pattern, cm, base, op=ALU.is_ge: step(pool.affine_select(
                out=v, in_=v, compare_op=op, fill=0.0, base=base, pattern=pattern, channel_multiplier=cm))
            step(pool.memset(ones[:, :], 1.0))
            for v, n in ((iota16, TOPK), (iota128, P)):
                step(pool.iota(v[:, :], pattern=[[1, n]], base=0, channel_multiplier=0, allow_small_or_imprecise_dtypes=True))
            step(pool.memset(ident[:, :], 0.0))
            step(pool.affine_select(out=ident[:, :], in_=ident[:, :], compare_op=ALU.not_equal, fill=1.0,
                                    base=0, pattern=[[-1, P]], channel_multiplier=1))
            step(pool.memset(headones[:, :], 0.0))
            for q in range(2):
                step(pool.memset(headones[CH * q:CH * q + CH, CH * q:CH * q + CH], 1.0))
            step(pool.memset(tri[:, :], 1.0))
            sel_ge(tri[:, :], [[1, P]], -1, 0)
            step(pool.memset(cst[:, 0:1], RMS_EPS))
            step(pool.memset(cst[:, 1:2], GN_EPS))
            step(pool.memset(cst[:, 2:3], 0.0))
            pool.memset(cst[:, 3:4], 1.0).then_inc(consts, 1)
            for n in range(2):
                split_lo(pool, n, n)
            pool.wait_ge(nl_ready, KT)
            for a in range(4):
                step(pool.memset(mask4[:, a, :], 0.0))
                for q in range(2):
                    step(pool.memset(mask4[CH * q:CH * q + CH, a, CH * q:CH * q + CH], 1.0))
                sel_ge(mask4[:, a, :], [[1, P]], -1, 0, ALU.is_gt if a % 2 == 0 else ALU.is_ge)
            for n, b in enumerate(LEVELS):
                step(pool.memset(lev[:, n, :], 0.0))
                v = lev[:, n, :].rearrange("p (q h u) -> p q h u", h=2, u=b)[:, :, 1, :]
                step(pool.memset(v, 1.0))
                q = P // (2 * b)
                sel_ge(v, [[-2 * b, q], [0, b]], 1, 0)
                sel_ge(v, [[2 * b, q], [0, b]], -1, b - 1)
            step(pool.memset(reset[:, :], 1.0))
            step(pool.memset(reset[:, :].rearrange("p (c u) -> p c u", u=CH)[:, :, 0:1], 0.0))
            for c in range(3):
                step(pool.memset(pin[c][:, 0:1], 0.0))
            pool.memset(Sh[:, :, :], 0.0).then_inc(consts, 1)
            for n in range(2, N_LORA):
                split_lo(pool, n, n % 2)
            with pool.Fori(0, (U_MLSTM - U_RWKV) // 2) as j:
                for c in range(2):
                    split_lo(pool, U_RWKV + 2 * j + c, c)
            pool.wait_ge(yr_stored, 16 * RJ)
            step(pool.memset(sel[:, :, :], 1.0))
            sel_ge(sel[:, :, :], [[-1, MH], [0, P]], 1, 0, ALU.is_ge)
            sel_ge(sel[:, :, :], [[1, MH], [0, P]], -1, 0, ALU.is_ge)
            for c in range(4):
                step(pool.memset(pc[c][:, 0:3], 0.0))
            pool.memset(rows[:, 7, :], 1.0).then_inc(consts, 1)
            with pool.Fori(0, (N_UNITS - U_MLSTM) // 2) as h:
                for c in range(2):
                    split_lo(pool, U_MLSTM + 2 * h + c, c)

        @block.scalar
        def _(act):
            step = Steps(act, act_step)
            st = {"norms": 0}

            def norm_act(Hs, sq, nt, ready, split=True):
                m = st["norms"]; st["norms"] += 1
                for k in range(KT):
                    ready(k)
                    if m * KT + k >= 2:
                        act.wait_ge(sq_used, m * KT + k - 1)
                    act.activation(sq[:, k % 2, :], Hs[:, k, :], ACT.Square).then_inc(sq_ready, 1)
                act.wait_ge(var_ready, m + 1)
                act.activation(rstd_of(m), rstd_of(m), ACT.Sqrt).then_inc(std_ready, 1)
                if split:
                    for k in range(KT):
                        act.wait_ge(nt_ready, m * KT + k + 1)
                        act.activation(xh[:, k, :], nt[:, k % 2, :], ACT.Copy).then_inc(nh_ready, 1)

            rstd_of = lambda m: (rstd1, rstd2, rstd3)[m][:, :]
            for n in range(2):
                split_hi(act, n, n, first=True)
            norm_act(H1, sq1, nt1, lambda k: act.wait_ge(x_in[k // 4], 16))
            act.wait_ge(consts, 2)
            for n in range(N_LORA):
                act.wait_ge(w_used, n + 1)
                if n:
                    act.wait_ge(lora_s, n)
                act.activation(plo[:, 1:T + 1], bank(6 + n % 2), ACT.Copy).then_inc(lora_p, 1)
                if n < 2:
                    act.wait_ge(lora_p, n + 1)
                    act.dma_start(if_d[n], plo[96:96 + MH, 1:T + 1]).then_inc(if_stored, 16)
                    act.wait_ge(if_stored, 16 * n + 16)
                act.wait_ge(lora_s, n + 1)
                f = (ACT.Tanh, ACT.Copy, ACT.Sigmoid, ACT.Sigmoid)[n]
                act.activation(lora[:, n, :], ysb[:, :], f).then_inc(lora_ready, 1)
                split_hi(act, n + 2, n % 2)

            def act_a(j, c, first=False):
                n = tile_unit(j, c)
                act.wait_ge(w_used, n + 1)
                if not first:
                    act.wait_ge(shifted, 3 * j)
                act.activation(pin[c][:, 1:T + 1], bank(6 + c % 2), ACT.Copy).then_inc(pin_saved, 1)
                split_hi(act, n + 2, c % 2)

            def act_side(n, s, dst, saved, stored):
                act.wait_ge(w_used, n + 1)
                act.wait_ge(sg_stored[s], 16 * stored + 16)
                own(act, act.activation(sgb[:, s, :], bank(6 + s), ACT.Sigmoid), side_saved, saved)
                act.dma_start(dst.rearrange("a p t -> p (a t)"), sgb[:, s, :]).then_inc(sg_stored[s], 16)
                split_hi(act, n + 2, s)

            def act_o(j, saved, stored):
                act_side(tile_unit(j, 3), 1, og_d[bass.ds(j, 1)], saved, stored)

            def act_gate(j, c, n, last=0):
                stored = 2 * j + c // 2
                act_side(n, c % 2, sg_d[bass.ds(4 * j + c, 1)], 5 * j + 3 - last + c,
                         stored + j + 2 - last if c % 2 else stored)

            def act_prep(j, a):
                act.wait_ge(lw_mm, 3 * j + 3)
                act.activation(sg, bank(0), ACT.Sigmoid, bias=rp(j, 3))
                act.activation(a_, bank(1), ACT.Sigmoid, bias=rp(j, 4))
                act.activation(g_sb[:, :], bank(2), ACT.Copy).then_inc(lw_taken, 1)
                act.wait_ge(cs_ready, j + 1)
                act.activation(E1, cs, ACT.Exp, scale=-DECAY)
                act.activation(E2, cs, ACT.Exp, scale=DECAY)
                act.activation(E0, E0, ACT.Exp, scale=-DECAY).then_inc(exps_ready, 1)
                a(0)
                act.wait_ge(kksum_ready, j + 1)
                act.activation(t1, bank(3), ACT.Sqrt).then_inc(kknorm_ready, 1)
                a(1)

            def act_b(j, follow):
                act.wait_ge(tr_ready, 4 * j + 2)
                act.activation(Vn[:, :, :].rearrange("p a b -> p (a b)"), bank(0), ACT.Copy).then_inc(tr_savedA, 1)
                act.activation(Bn[:, :, :].rearrange("p a b -> p (a b)"), bank(1), ACT.Copy).then_inc(tr_savedA, 1)
                follow(F_TR + 4 * F_INTRA)
                for q in range(2):
                    act.wait_ge(x0_ready, 2 * j + q + 1)
                    act.activation(X[:, 4 * q:4 * q + 4, :], bank(q), ACT.Copy).then_inc(x0_saved, 1)
                follow(F_X0)
                for n in range(1, len(LEVELS)):
                    follow(F_LEVEL)
                    if n < len(LEVELS) - 1:
                        for q in range(2):
                            act.wait_ge(xx_ready, 2 * (4 * j + n - 1) + q + 1)
                            act.activation(X[:, 4 * q:4 * q + 4, :], bank(2 + q), ACT.Copy).then_inc(x_saved, 1)
                    follow(F_LEVEL)
                act.wait_ge(wt_ready, j + 1)
                act.activation(WT[:, :], bank(0), ACT.Copy).then_inc(wt_saved, 1)
                follow(F_W)
                act.wait_ge(g_ready, j + 1)
                act.activation(Gn[:, :, :, :], ps[:, 2:4, :].rearrange("p b (n c) -> p b n c", n=TT)[:, :, :, 0:CH], ACT.Copy).then_inc(g_saved, 1)
                follow(F_G)
                for c in range(NCH):
                    follow(F_U)
                    follow(F_S)
                act.wait_ge(s_saved, NCH * j + NCH)
                act.wait_ge(y_ready, j + 1)
                act.activation(ysb[:, :], bank(0), ACT.Copy).then_inc(y_saved, 1)
                act.wait_ge(yvar_ready, j + 1)
                act.activation(ysq[:, :], bank(5), ACT.Sqrt, scale=1.0 / CH, bias=cst[:, 1:2]).then_inc(ystd_ready, 1)
                act.wait_ge(yo_ready, j + 1)
                act.dma_start(yr_d[bass.ds(j, 1)].rearrange("a p t -> p (a t)"), ysb[:, :]).then_inc(yr_stored, 16)

            for s in range(2):
                act.sem_inc(sg_stored[s], 16)
            for c in range(3):
                act_a(0, c, first=True)
            act_o(0, 1, 0)
            with act.Fori(1, RJ) as i:
                def save(c):
                    if c == 0:
                        act_a(i, 2)
                    elif c == 1:
                        act_o(i, 5 * i - 3, 3 * i - 2)
                    else:
                        act_gate(i - 1, c - 2, tile_unit(i, c + 2))

                act_prep(i - 1, lambda c: act_a(i, c))
                act_b(i - 1, Follower(6, save))
                act.wait_ge(yr_stored, 16 * (i - 1) + 16)
            j = RJ - 1
            act_prep(j, lambda c: None)
            act_b(j, Follower(N_SIDE, lambda c: act_gate(j, c, U_MLSTM - N_SIDE + c, last=1)))
            act.wait_ge(yr_stored, 16 * RJ)

            act.wait_ge(lf_e, 1)
            act.activation(rows[:, 3, :], rows[:, 2, :], ACT.Exp, scale=-1.0).then_inc(lf_ln, 1)
            act.wait_ge(lf_ln, 1)
            act.activation(rows[:, 4, :], rows[:, 3, :], ACT.Ln, bias=cst[0:MH, 3:4]).then_inc(lf_ln, 1)
            act.wait_ge(lf_e, 2)
            act.activation(rows[:, 4, :], rows[:, 6, :], ACT.Exp, scale=-1.0).then_inc(nm_ready, 1)
            for h in range(MH):
                for c in range(2):
                    act.wait_ge(rb_ready, 2 * h + c + 1)
                    act.activation(RNb[:, h, c, :], bank(2 + c), ACT.Copy).then_inc(rb_saved, 1)

            def act_m(h, first=False):
                n = U_MLSTM + 6 * h
                if not first:
                    act_att(h - 1)
                for c in range(4):
                    act.wait_ge(w_used, n + c + 1)
                    if not first:
                        act.wait_ge(conv_ready, 4 * h + c - 3)
                    act.activation(pc[c][:, 3:T + 3], bank(6 + c % 2), ACT.Copy).then_inc(pc_saved, 1)
                    split_hi(act, n + c + 2, c % 2)
                    if not first and c == 0:
                        act.wait_ge(sc_ready, TT * h)
                    act.wait_ge(conv_ready, 4 * h + c + 1)
                    act.activation(QK[:, c, :], cacc[:, c % 2, :], ACT.Silu).then_inc(qk_ready, 1)
                    if not first and c == 2:
                        act_att_store(h - 1)
                act.wait_ge(w_used, n + 5)
                split_hi(act, n + 6, 0)
                act.wait_ge(w_used, n + 6)
                if not first:
                    act.wait_ge(hm_ready, h)
                for c in range(2):
                    act.activation(Vm[:, 2 * c:2 * c + 2, :].rearrange("p a b -> p (a b)"), bank(c), ACT.Copy).then_inc(v_saved, 1)
                split_hi(act, n + 7, 1)

            def act_att(h):
                act.wait_ge(arg_ready, h + 1)
                for i in range(TT):
                    act.activation(Dm[:, i, P * i:T], Dm[:, i, P * i:T], ACT.Exp, scale=-1.0).then_inc(dm_ready, 1)

            def act_att_store(h):
                act.wait_ge(ym_ready, h + 1)
                act.dma_start(ym_d[bass.ds(2 * h, 2)].rearrange("a p t -> p a t"), ymo[:, :, :]).then_inc(ym_stored, 16)

            def load_og(h):
                act.dma_start(og[:, :, :], og_d[bass.ds(2 * h, 2)].rearrange("a p t -> p a t")).then_inc(og_in, 16)

            act_m(0, first=True)
            with act.Fori(1, MH) as h:
                load_og(h - 1)
                act_m(h)
                act.wait_ge(ym_stored, 16 * h)
            load_og(MH - 1)
            act_att(MH - 1)
            act_att_store(MH - 1)
            act.wait_ge(ym_stored, 16 * MH)

            for c in range(4):
                src = (ym_d, yr_d)[c // 2][4 * (c % 2):4 * (c % 2) + 4]
                if c:
                    act.wait_ge(yl_ready, c)
                act.dma_start(yraw[:, :, :], src.rearrange("k p t -> p k t")).then_inc(yraw_in, 16)
                act.wait_ge(yraw_in, 16 * c + 16)
                act.activation(yh[:, 4 * c:4 * c + 4, :], yraw[:, :, :], ACT.Copy).then_inc(yh_ready, 1)

            def act_mix(d, dd):
                split_hi(act, U_MIX + 2 * d + dd + 2, dd)
                act.wait_ge(mix_ready, 2 * d + dd + 1)
                act.activation(xh[:, bass.ds(2 * d + dd, 1), :].rearrange("p a t -> p (a t)"), mxo[:, dd, :], ACT.Copy).then_inc(mh_ready, 1)

            with act.Fori(0, KT // 2) as d:
                for dd in range(2):
                    act_mix(d, dd)
            act.wait_ge(w_used, U_OUT)
            act.wait_ge(ml_ready, KT)
            for c in range(4):
                act.dma_start(H[:, 4 * c:4 * c + 4, :], x_t[4 * c:4 * c + 4].rearrange("k p t -> p k t")).then_inc(h_in, 16)
            with act.Fori(0, KT // 2 - 1) as d:
                for c in range(2):
                    split_hi(act, U_OUT + 2 * d + c + 2, c)
            norm_act(H, sq2, nt2, lambda k: (
                act.wait_ge(h_ready, k + 1),
                split_hi(act, U_QUERY + k - KT + 2, k % 2) if k >= KT - 2 else None))
            act.dma_start(keys[:, :, :], keys_t).then_inc(keys_in, 16)

            def act_ahead(e, s, n):
                act.wait_ge(w_used, n + 1)
                act.wait_ge(pre_stored[s], 8 * e + 16 - 8 * s)
                own(act, act.activation(preb[:, s, :], bank(4 + s), ACT.Gelu), pre_ready, e + 1)
                act.dma_start(act_d[bass.ds(e, 1)].rearrange("a p t -> p (a t)"), preb[:, s, :]).then_inc(pre_stored[s], 16)
                split_hi(act, n + 2, s)

            def act_route(h, first=False):
                n = U_QUERY + 4 * h
                for c in range(2):
                    act.wait_ge(w_used, n + c + 1)
                    if not first:
                        act.wait_ge(key_scores, 2 * h + c - 1)
                    act.activation(qsb[:, c, :], bank(c), ACT.Copy).then_inc(q_saved, 1)
                    split_hi(act, n + c + 2, c)
                for c in range(2):
                    act.wait_ge(key_scores, 2 * h + c + 1)
                    if not first:
                        act.wait_ge(sel_done, 2 * h + c - 1)
                    act.activation(ssb[:, c, :, :].rearrange("p a b -> p (a b)"), bank(2 + c), ACT.Copy).then_inc(ssb_saved, 1)
                    act_ahead(2 * h + c, c, n + 2 + c)

            def act_softmax(h):
                act.wait_ge(best_ready, h + 1)
                act.activation(ex[:, :, :], ex[:, :, :], ACT.Exp).then_inc(ex_ready, 1)

            for s in range(2):
                act.sem_inc(pre_stored[s], 16)
            act_route(0, first=True)
            with act.Fori(1, HEADS) as h:
                act_route(h)
                act_softmax(h - 1)
            for e in range(2 * HEADS, 2 * AHEAD):
                if e == 2 * AHEAD - 1:
                    act_softmax(HEADS - 1)
                act_ahead(e, e % 2, U_TAIL + e - 2 * HEADS)
            for m in range(3):
                act.wait_ge(egt_ready, m + 1)
                act.activation(EGT[:, m, :], bank(4 + m), ACT.Copy).then_inc(egt_saved, 1)
            for s in range(2):
                act.wait_ge(pre_stored[s], 16 * (AHEAD + 1))
            def act_dense(b, s, first=False):
                if not first:
                    act.wait_ge(gates_stored[s], 8 * b - 8 * s)
                with act.Fori(0, GT // 16) as q:
                    for c in range(4):
                        act.wait_ge(oh_used, GT * b + 16 * q + 4 * c + 4)
                        act.activation(stage[s][:, :, bass.ds(16 * q + 4 * c, 4)].rearrange("p e t -> p t e"),
                                       bank(c).rearrange("p (t e) -> p t e", t=4), ACT.Copy).then_inc(dense_saved, 1)
                act.wait_ge(dense_saved, (GT // 4) * (b + 1))
                act.dma_start(gate_d[bass.ds(b, 1)].rearrange("a p e t -> p (a e t)"),
                              stage[s][:, :, :].rearrange("p e t -> p (e t)")).then_inc(gates_stored[s], 16)

            for s in range(2):
                act_dense(s, s, first=True)
            with act.Fori(1, GB // 2) as b:
                for s in range(2):
                    act_dense(2 * b + s, s)
            for s in range(2):
                act.wait_ge(gates_stored[s], 8 * GB)

            def load_gates(g):
                for e in range(2):
                    act.dma_start(gt[:, e, :].rearrange("p (b t) -> p b t", b=GB),
                                  gate_d[:, :, bass.ds(2 * g + e, 1), :].rearrange("b p a t -> p b (a t)")).then_inc(gt_in, 16)

            def act_halves(g, s):
                for e in range(2):
                    act.wait_ge(ga_ready, 2 * g + e + 1)
                    act.activation(gah[s][:, e, :], act_[:, e, :], ACT.Copy).then_inc(gah_ready, 1)

            def act_fetch(g, s, first=False):
                load_gates(g)
                if not first:
                    act.wait_ge(gal_ready, 2 * g)
                act.dma_start(act_[:, :, :], act_d[bass.ds(2 * g, 2)].rearrange("a p t -> p a t")).then_inc(pre_in, 16)
                act_halves(g, s)

            def act_scores(g, s, n0):
                load_gates(g)
                for e in range(2):
                    act.wait_ge(w_used, n0 + e + 1)
                    act.wait_ge(gal_ready, 2 * g + e - 1)
                    act.activation(act_[:, e, :], bank(e), ACT.Gelu).then_inc(gelu_ready, 1)
                    split_hi(act, n0 + e + 2, e)
                act_halves(g, s)

            def act_values(n0, last=False):
                for e in range(2):
                    act.wait_ge(w_used, n0 + e + 1)
                    split_hi(act, n0 + e + 2, e)

            act_fetch(0, 0, first=True)
            act_fetch(1, 1)
            act_values(U_PEER)
            with act.Fori(1, AHEAD // 2) as i:
                for s in range(2):
                    act_fetch(2 * i + s, s)
                    act_values(U_PEER + 2 * (2 * i + s - 1))
            with act.Fori(AHEAD // 2, GROUPS // 2) as i:
                for s in range(2):
                    g = 2 * i + s
                    act_scores(g, s, U_SCORED + 4 * (g - AHEAD))
                    act_values(U_SCORED + 4 * (g - AHEAD) + 2)
            norm_act(H, sq3, None, lambda k: act.wait_ge(out_added, KT * (GROUPS - 1) + k + 1), split=False)

        @block.vector
        def _(dve):
            step = Steps(dve, dve_step)
            st = {"norms": 0}
            rstd_of = lambda m: (rstd1, rstd2, rstd3)[m][:, :]

            def norm_dve(Hs, nt, gain):
                m = st["norms"]; st["norms"] += 1
                dve.wait_ge(sq_used, (m + 1) * KT)
                dve.tensor_scalar(rstd_of(m), bank(7), 1.0 / D, RMS_EPS, ALU.mult, ALU.add).then_inc(var_ready, 1)
                dve.wait_ge(std_ready, m + 1)
                step(dve.reciprocal(rstd_of(m), rstd_of(m)))

                def normed(k):
                    if k >= 2:
                        dve.wait_ge(nl_ready, m * KT + k - 1)
                    dve.scalar_tensor_tensor(nt[:, k % 2, :], Hs[:, k, :], par[:, C_GAIN + m * KT + k:C_GAIN + m * KT + k + 1],
                                             rstd_of(m), ALU.mult, ALU.mult).then_inc(nt_ready, 1)
                normed(0)
                for k in range(KT):
                    if k + 1 < KT:
                        normed(k + 1)
                    dve.wait_ge(nh_ready, m * KT + k + 1)
                    dve.tensor_tensor(xl[:, k, :], nt[:, k % 2, :], xh[:, k, :].bitcast(F32), ALU.subtract).then_inc(nl_ready, 1)

            dve.wait_ge(par_in, 16)
            norm_dve(H1, nt1, 0)
            dve.wait_ge(consts, 2)

            def shift(dst, src, mu, signal, count):
                step(dve.tensor_tensor(t1, src[:, 0:T], src[:, 1:T + 1], ALU.subtract))
                own(dve, dve.scalar_tensor_tensor(dst, t1, mu, src[:, 1:T + 1], ALU.mult, ALU.add), signal, count)

            for n in range(N_LORA):
                dve.wait_ge(lora_p, n + 1)
                if n:
                    dve.wait_ge(lora_ready, n)
                shift(ysb[:, :], plo, par[:, C_LMU + n:C_LMU + n + 1], lora_s, n + 1)

            def dve_prep(j):
                dve.wait_ge(pin_saved, 3 * j + 3)
                for c, dst in enumerate((r_, k_, v_)):
                    shift(dst, pin[c], rp(j, c), shifted, 3 * j + c + 1)
                step(dve.tensor_scalar(kk, k_, rp(j, 5), None, ALU.mult))
                own(dve, dve.tensor_tensor(t2, kk, kk, ALU.mult), kk_ready, j + 1)
                dve.wait_ge(lw_taken, j + 1)
                step(dve.tensor_tensor_scan(cs, reset[:, :], sg, 0.0, ALU.mult, ALU.add))
                own(dve, dve.tensor_tensor(E0, cs, sg, ALU.subtract), cs_ready, j + 1)
                step(dve.tensor_scalar(sg, a_, 1.0, rp(j, 6), ALU.subtract, ALU.mult))
                step(dve.scalar_tensor_tensor(k_, sg, 1.0, k_, ALU.add, ALU.mult))
                dve.wait_ge(kksum_ready, j + 1)
                own(dve, dve.scalar_tensor_tensor(t2, r_, rp(j, 7), k_, ALU.mult, ALU.mult), bprod_ready, j + 1)
                dve.wait_ge(exps_ready, j + 1)
                step(dve.tensor_tensor(AR[:, 1, :], r_, E1, ALU.mult))
                step(dve.tensor_tensor(Kt[:, :], k_, E2, ALU.mult))
                step(dve.tensor_copy(EL[:, :], E1.rearrange("p (c u) -> p c u", u=CH)[:, :, CH - 1]))
                dve.wait_ge(kknorm_ready, j + 1)
                step(dve.tensor_scalar(t1, t1, L2_EPS, None, ALU.max))
                step(dve.reciprocal(sg, t1))
                step(dve.tensor_tensor(kk, kk, sg, ALU.mult))
                step(dve.scalar_tensor_tensor(AR[:, 0, :], kk, -1.0, E0, ALU.mult, ALU.mult))
                step(dve.tensor_tensor(kk, kk, a_, ALU.mult))
                step(dve.tensor_tensor(Bt[:, :], kk, E2, ALU.mult))
                dve.wait_ge(bsum_ready, j + 1)
                dve.tensor_tensor(bonus[:, :], bank(4), v_, ALU.mult).then_inc(prep_done, 1)
                dve.wait_ge(prep_done, j + 1)

            idb = ident[:, :].unsqueeze(1).to_broadcast([P, 8, P])

            def level_mask(n):
                return lev[:, n, :].unsqueeze(1).to_broadcast([P, 8, P])

            def dve_b(j):
                dve.wait_ge(tr_ready, 4 * j + 4)
                dve.tensor_copy(Kn[:, :, :].rearrange("p a b -> p (a b)"), bank(2)).then_inc(tr_savedD, 1)
                dve.tensor_copy(An[:, :, :].rearrange("p a b -> p (a b)"), bank(3)).then_inc(tr_savedD, 1)
                for m in range(8):
                    dve.wait_ge(intra_ready, 8 * j + m + 1)
                    dve.tensor_tensor(M4[:, m, :, :], bank(4 + m % 2).rearrange("p (a t) -> p a t", a=4), mask4[:, :, :],
                                      ALU.mult).then_inc(intra_saved, 1)
                dve.wait_ge(intra_saved, 8 * j + 8)
                step(dve.tensor_tensor(XT[:, :, :], M4[:, :, 0, :], level_mask(0), ALU.mult))
                dve.tensor_tensor(XT[:, :, :], XT[:, :, :], idb, ALU.add).then_inc(xt0_ready, 1)
                own(dve, dve.tensor_tensor(Mb[:, :, :], M4[:, :, 0, :], level_mask(1), ALU.mult), mb_ready, 5 * j + 1)
                for n in range(1, len(LEVELS)):
                    m = 5 * j + n - 1
                    for q in range(2):
                        dve.wait_ge(z_ready, 2 * m + q + 1)
                        dve.tensor_tensor(Z[:, 4 * q:4 * q + 4, :], bank(q).rearrange("p (a t) -> p a t", a=4), idb[:, 0:4, :],
                                          ALU.add).then_inc(z_saved, 1)
                    if n + 1 < len(LEVELS):
                        dve.tensor_tensor(Mb[:, :, :], M4[:, :, 0, :], level_mask(n + 1), ALU.mult).then_inc(mb_ready, 1)
                    for q in range(2):
                        dve.wait_ge(xt_ready, 2 * m + q + 1)
                        dve.tensor_copy(XT[:, 4 * q:4 * q + 4, :], bank(4 + q).rearrange("p (a t) -> p a t", a=4)).then_inc(xt_saved, 1)
                dve.wait_ge(akv_ready, j + 1)
                v = ps[:, 4:6, :].rearrange("p b (n h c) -> p b n h c", n=TT, h=2)
                for h in range(2):
                    last = dve.tensor_copy(AKV[:, h, :, :], v[:, h, :, h, :])
                    last.then_inc(akv_saved, 1)
                dve.wait_ge(g_saved, j + 1)
                for c in range(NCH):
                    tt, q = divmod(c, 2)
                    rows_ = slice(CH * q, CH * q + CH)
                    dve.wait_ge(u_ready, NCH * j + c + 1)
                    dve.tensor_tensor(Un[rows_, tt, :, :], bank(3)[rows_, 0:P].rearrange("p (h c) -> p h c", h=2),
                                      Gn[rows_, :, tt, :], ALU.add).then_inc(u_saved, 1)
                    step(dve.tensor_scalar(SE[:, :], Sh[:, c, :], EL[:, c:c + 1], None, ALU.mult))
                    dve.wait_ge(s_ready, NCH * j + c + 1)
                    step(dve.scalar_tensor_tensor(Sh[0:CH, c + 1, 0:CH], bank(4)[0:CH, 0:CH], EL[0:CH, c:c + 1], SE[0:CH, 0:CH],
                                                  ALU.mult, ALU.add))
                    own(dve, dve.scalar_tensor_tensor(Sh[CH:P, c + 1, CH:P], bank(4)[CH:P, CH:P], EL[CH:P, c:c + 1], SE[CH:P, CH:P],
                                                      ALU.mult, ALU.add), s_saved, NCH * j + c + 1)
                dve.wait_ge(y_saved, j + 1)
                dve.wait_ge(mean_ready, j + 1)
                step(dve.scalar_tensor_tensor(yc[:, :], bank(1), -1.0 / CH, ysb[:, :], ALU.mult, ALU.add))
                own(dve, dve.tensor_tensor(ysq[:, :], yc[:, :], yc[:, :], ALU.mult), ysq_ready, j + 1)
                dve.wait_ge(ystd_ready, j + 1)
                step(dve.reciprocal(ysb[:, :], ysq[:, :]))
                step(dve.tensor_tensor(yc[:, :], yc[:, :], ysb[:, :], ALU.mult))
                step(dve.tensor_scalar(yc[:, :], yc[:, :], rp(j, 8), rp(j, 9), ALU.mult, ALU.add))
                step(dve.tensor_tensor(yc[:, :], yc[:, :], bonus[:, :], ALU.add))

            def dve_y(j):
                own(dve, dve.tensor_tensor(ysb[:, :], yc[:, :], g_sb[:, :], ALU.mult), yo_ready, j + 1)

            with dve.Fori(0, RJ) as j:
                step.enter(j, 0, STEPS_RWKV)
                dve_prep(j)
                dve_b(j)
                dve_y(j)
                step.leave(RJ)

            dve.wait_ge(consts, 3)
            dve.wait_ge(rows_in, 32)
            row = lambda n: rows[:, n, :]
            step(dve.tensor_scalar(row(0), row(0), par[0:MH, C_BI:C_BI + 1], None, ALU.add))
            step(dve.tensor_scalar(row(1), row(1), par[0:MH, C_BI + 1:C_BI + 2], None, ALU.add))
            own(dve, dve.scalar_tensor_tensor(row(2), row(1), -1.0, row(1), ALU.mult, ALU.max), lf_e, 1)
            step(dve.tensor_scalar(row(1), row(1), 0.0, None, ALU.min))
            dve.wait_ge(lf_ln, 2)
            step(dve.tensor_tensor(row(1), row(1), row(4), ALU.subtract))
            step(dve.tensor_tensor_scan(row(2), row(7), row(1), 0.0, ALU.mult, ALU.add))
            dve.tensor_tensor(row(3), row(0), row(2), ALU.subtract).then_inc(rows_ready, 1)
            dve.wait_ge(rows_ready, 1)
            step(dve.tensor_tensor_scan(row(5), row(7), row(3), 0.0, ALU.mult, ALU.max))
            dve.tensor_tensor(row(6), row(2), row(5), ALU.add).then_inc(lf_e, 1)
            dve.wait_ge(lf_e, 2)
            dve.wait_ge(rc_ready, 1)
            step(dve.tensor_copy(rcol[:, :, :].rearrange("p a b -> p (a b)"), bank(4)[:, 0:TT * MH]))
            dve.wait_ge(rb_saved, 2 * MH)

            def conv(h, c, first=False):
                t = [h * 2, h * 2 + 1, 8 + h * 2, 8 + h * 2 + 1][c]
                w = lambda u: par[:, bass.ds(C_CONV + 4 * t + u, 1)]
                dve.wait_ge(pc_saved, 4 * h + c + 1)
                if c >= 2:
                    dve.wait_ge(qk_ready, 4 * h + c - 1)
                elif not first:
                    dve.wait_ge(qk_ready, 4 * h + c - 1)
                a = cacc[:, c % 2, :]
                step(dve.tensor_scalar(a, pc[c][:, 0:T], w(0), None, ALU.mult))
                for u in range(1, 3):
                    step(dve.scalar_tensor_tensor(a, pc[c][:, u:u + T], w(u), a, ALU.mult, ALU.add))
                dve.scalar_tensor_tensor(a, pc[c][:, 3:T + 3], w(3), a, ALU.mult, ALU.add).then_inc(conv_ready, 1)
                dve.wait_ge(conv_ready, 4 * h + c + 1)

            def dve_args(h):
                for i in range(TT):
                    last = dve.tensor_scalar(Dm[:, i, P * i:T], RNb[:, bass.ds(h, 1), 0, P * i:T].rearrange("p a t -> p (a t)"),
                                             rcol[:, i, bass.ds(h, 1)], 0.0, ALU.subtract, ALU.max)
                last.then_inc(arg_ready, 1)

            SC = [(2, 0), (3, 0), (4, 0), (3, 384)]

            def dve_weights(h):
                dve.wait_ge(sc_ready, TT * h + TT)
                dve.wait_ge(dm_ready, TT * h + TT)
                for i in range(TT):
                    lo = P * i
                    b, at = SC[i]
                    step(dve.scalar_tensor_tensor(SD[:, i, lo:T], bank(b)[:, at:at + T - lo], 1.0 / 16.0, Dm[:, i, lo:T],
                                                  ALU.mult, ALU.mult))
                    dve.tensor_tensor(SD[:, i, lo:lo + P], SD[:, i, lo:lo + P], tri[:, :], ALU.mult).then_inc(sd_ready, 1)

            def dve_heads(h):
                dve.wait_ge(hm_ready, h + 1)
                step(dve.scalar_tensor_tensor(rec[:, :], bank(3), -1.0, RNb[:, bass.ds(h, 1), 1, :].rearrange("p a t -> p (a t)"),
                                              ALU.mult, ALU.max))
                step(dve.tensor_tensor(rec[:, :], bank(3), rec[:, :], ALU.max))
                step(dve.reciprocal(rec[:, :], rec[:, :]))
                for c in range(2):
                    step(dve.tensor_tensor(hv[:, c, :], bank((5, 2)[c]), rec[:, :], ALU.mult))
                dve.wait_ge(og_in, 16 * h + 16)
                own(dve, dve.tensor_tensor(ymo[:, :, :], hv[:, :, :], og[:, :, :], ALU.mult), ym_ready, h + 1)

            for c in range(4):
                conv(0, c, first=True)
            with dve.Fori(1, MH) as h:
                step.enter(h, 1, STEPS_MLSTM)
                dve_args(h - 1)
                conv(h, 0)
                dve_weights(h - 1)
                conv(h, 1)
                dve_heads(h - 1)
                conv(h, 2)
                conv(h, 3)
                step.leave(MH - 1)
            dve_args(MH - 1)
            dve_weights(MH - 1)
            dve_heads(MH - 1)

            dve.wait_ge(ym_stored, 16 * MH)
            for c in range(4):
                dve.wait_ge(yh_ready, c + 1)
                dve.tensor_tensor(yl[:, 4 * c:4 * c + 4, :], yraw[:, :, :], yh[:, 4 * c:4 * c + 4, :].bitcast(F32), ALU.subtract).then_inc(yl_ready, 1)
            def merge(d, dd):
                k = 2 * d + dd
                dve.wait_ge(sg_in[dd], 32 * d + 32)
                dve.wait_ge(w_used, U_MIX + k + 1)
                for c in range(2):
                    step(dve.tensor_tensor(sgm[:, dd, c, :], bank(2 * dd + c), sgm[:, dd, c, :], ALU.mult))
                own(dve, dve.tensor_tensor(mxo[:, dd, :], sgm[:, dd, 0, :], sgm[:, dd, 1, :], ALU.add), mix_ready, k + 1)
                dve.wait_ge(mh_ready, k + 1)
                at = lambda t: t[:, bass.ds(k, 1), :].rearrange("p a t -> p (a t)")
                own(dve, dve.tensor_tensor(at(xl), mxo[:, dd, :], at(xh).bitcast(F32), ALU.subtract), ml_ready, k + 1)

            with dve.Fori(0, KT // 2) as d:
                step.enter(d, 0, 4)
                for dd in range(2):
                    merge(d, dd)
                step.leave(KT // 2)
            dve.wait_ge(h_in, 64)
            with dve.Fori(0, KT // 2) as d:
                for c in range(2):
                    dve.wait_ge(w_used, U_OUT + 2 * d + c + 1)
                    hk = H[:, bass.ds(2 * d + c, 1), :].rearrange("p a t -> p (a t)")
                    dve.tensor_tensor(hk, bank(c), hk, ALU.add).then_inc(h_ready, 1)
            norm_dve(H, nt2, 1)

            def top16(vals, idx, src, rep):
                dve.sem_inc(passed, 1)
                step(dve.max(vals[:, 0:8], src))
                dve.sem_inc(passed, 1)
                step(dve.max_index(idx[:, 0:8], vals[:, 0:8], src))
                dve.sem_inc(passed, 1)
                step(dve.match_replace(rep, vals[:, 0:8], src, -3.0e38))
                dve.sem_inc(passed, 1)
                step(dve.max(vals[:, 8:16], rep))
                dve.sem_inc(passed, 1)
                step(dve.max_index(idx[:, 8:16], vals[:, 8:16], rep))

            with dve.Fori(0, HEADS) as h:
                step.enter(h, 0, STEPS_ROUTE)
                for c in range(2):
                    dve.wait_ge(ssb_saved, 2 * h + c + 1)
                    for tt in range(TT):
                        top16(v16[:, c, tt, :], i16[:, c, tt, :], ssb[:, c, tt, :], srep[:, :])
                    dve.tensor_copy(if16[:, c, :, :], i16[:, c, :, :]).then_inc(sel_done, 1)
                dve.wait_ge(sel_done, 2 * h + 2)
                for tt in range(TT):
                    c3 = lambda t: t[:, :].rearrange("p (a b) -> p a b", a=TOPK)
                    step(dve.tensor_tensor(c3(cand), v16[:, 0, tt, :].unsqueeze(2).to_broadcast([P, TOPK, TOPK]),
                                           v16[:, 1, tt, :].unsqueeze(1).to_broadcast([P, TOPK, TOPK]), ALU.add))
                    top16(best[:, tt, :], ci[:, tt, :], cand[:, :], crep[:, :])
                dve.tensor_tensor(ex[:, :, :], best[:, :, :], best[:, :, 0:1].to_broadcast([P, TT, TOPK]), ALU.subtract).then_inc(best_ready, 1)
                step(dve.tensor_scalar(chi[:, 0, :, :], ci[:, :, :], 4, None, ALU.logical_shift_right))
                step(dve.tensor_scalar(chi[:, 1, :, :], ci[:, :, :], 15, None, ALU.bitwise_and))
                step(dve.tensor_copy(chf[:, :, :, :], chi[:, :, :, :]))
                for tt in range(TT):
                    for c in range(2):
                        step(dve.tensor_tensor(eq[:, :, :], chf[:, c, tt, :].unsqueeze(2).to_broadcast([P, TOPK, TOPK]),
                                               iota16[:, :].unsqueeze(1).to_broadcast([P, TOPK, TOPK]), ALU.is_equal))
                        step(dve.tensor_tensor(eq[:, :, :], eq[:, :, :], if16[:, c, tt, :].unsqueeze(1).to_broadcast([P, TOPK, TOPK]), ALU.mult))
                        step(dve.tensor_reduce(EG[:, c, tt, bass.ds(TOPK * h, TOPK)], eq[:, :, :], AX.X, ALU.add))
                dve.wait_ge(ex_ready, h + 1)
                step(dve.tensor_reduce(sm[:, 0, :], ex[:, :, :], AX.X, ALU.add))
                step(dve.reciprocal(sm[:, 1, :], sm[:, 0, :]))
                dve.tensor_tensor(EG[:, 2, :, bass.ds(TOPK * h, TOPK)], ex[:, :, :], sm[:, 1, :].unsqueeze(2).to_broadcast([P, TT, TOPK]),
                                  ALU.mult).then_inc(routed, 1)
                dve.wait_ge(routed, h + 1)
                step.leave(HEADS)
            dve.wait_ge(egt_saved, 3)

            def onehots(i, u, first=False):
                s = u % OH
                t = lambda m: EGT[:, m, bass.ds(16 * i + u, 1)]
                if not (first and u < OH):
                    dve.wait_ge(oh_used, 16 * i + u - OH + 1)
                dve.tensor_scalar(oh[s][0][:, :], iota128[:, :], t(1), None, ALU.is_equal)
                dve.tensor_scalar(oh[s][1][:, :], iota128[:, :], t(0), t(2), ALU.is_equal, ALU.mult).then_inc(oh_ready, 1)

            for u in range(16):
                onehots(0, u, first=True)
            with dve.Fori(1, T // 16) as i:
                for u in range(16):
                    onehots(i, u)

            def dve_gated(g, s, ahead):
                dve.wait_ge(gt_in, 32 * g + 32)
                if ahead:
                    dve.wait_ge(pre_in, 16 * g + 16)
                for e in range(2):
                    if not ahead:
                        dve.wait_ge(gelu_ready, 2 * (g - AHEAD) + e + 1)
                    dve.tensor_tensor(act_[:, e, :], act_[:, e, :], gt[:, e, :], ALU.mult).then_inc(ga_ready, 1)
                for e in range(2):
                    dve.wait_ge(gah_ready, 2 * g + e + 1)
                    dve.tensor_tensor(gal[s][:, e, :], act_[:, e, :], gah[s][:, e, :].bitcast(F32), ALU.subtract).then_inc(gal_ready, 1)

            def dve_values(g, n0):
                for d in range(KT):
                    if d % 8 == 7:
                        dve.wait_ge(w_used, n0 + d // 8 + 1)
                    else:
                        dve.wait_ge(out_ready, 14 * g + d - d // 8 + 1)
                    dve.tensor_tensor(H[:, d, :], bank(2 + d % 4), H[:, d, :], ALU.add).then_inc(out_added, 1)

            dve_gated(0, 0, True)
            dve_gated(1, 1, True)
            dve_values(0, U_PEER)
            with dve.Fori(1, AHEAD // 2) as i:
                for s in range(2):
                    g = 2 * i + s
                    dve_gated(g, s, True)
                    dve_values(g - 1, U_PEER + 2 * (g - 1))
            with dve.Fori(AHEAD // 2, GROUPS // 2) as i:
                for s in range(2):
                    g = 2 * i + s
                    dve_gated(g, s, False)
                    dve_values(g - 1, U_SCORED + 4 * (g - AHEAD) + 2)
            dve_values(GROUPS - 1, N_UNITS - 2)
            m = st["norms"]
            dve.wait_ge(sq_used, (m + 1) * KT)
            dve.tensor_scalar(rstd_of(m), bank(7), 1.0 / D, RMS_EPS, ALU.mult, ALU.add).then_inc(var_ready, 1)
            dve.wait_ge(std_ready, m + 1)
            step(dve.reciprocal(rstd_of(m), rstd_of(m)))
            for k in range(KT):
                c = C_GAIN + m * KT + k
                dve.scalar_tensor_tensor(H[:, k, :], H[:, k, :], par[:, c:c + 1], rstd_of(m), ALU.mult, ALU.mult).then_inc(last_ready, 1)

        @block.tensor
        def _(pe):
            st = {"norms": 0}

            def norm_pe(sq):
                m = st["norms"]; st["norms"] += 1
                for k in range(KT):
                    pe.wait_ge(sq_ready, m * KT + k + 1)
                    pe.matmul(bank(7), ones[:, :], sq[:, k % 2, :], start=k == 0, stop=k == KT - 1).then_inc(sq_used, 1)

            def first_unit(n, s, dst, m):
                pe.wait_ge(w_lo, n + 1)
                for k in range(KT):
                    pe.wait_ge(nl_ready, m * KT + k + 1)
                    last = products(pe, dst, s, k, P, xh, xl, k, k == 0, k == KT - 1)
                last.then_inc(w_used, 1)

            pe.wait_ge(consts, 1)
            norm_pe(sq1)
            first_unit(0, 0, bank(6), 0)
            for n in range(1, N_LORA):
                if n >= 2:
                    pe.wait_ge(lora_p, n - 1)
                unit(pe, n, n % 2, bank(6 + n % 2))

            def unit_waits(i, c):
                if isinstance(i, int) and i == 0:
                    pe.wait_ge(lora_p, 3 + c) if c < 2 else pe.wait_ge(pin_saved, c - 1)
                elif c < 2:
                    pe.wait_ge(side_saved, 5 * i - 4)
                elif c < 5:
                    pe.wait_ge(pin_saved, 3 * i + c - 1)
                else:
                    pe.wait_ge(side_saved, 5 * i - 8 + c)

            def pe_prep(j, i):
                pe.wait_ge(lw_in, 16 * j + 16)
                pe.wait_ge(lora_ready, N_LORA)
                pe.matmul(bank(0), lw[:, 0, :], lora[:, 0, :], start=True, stop=True).then_inc(lw_mm, 1)
                pe.matmul(bank(1), lw[:, 1, :], lora[:, 1, :], start=True, stop=True).then_inc(lw_mm, 1)
                pe.matmul(bank(2), lw[:, 2, :], lora[:, 2, :], start=True, stop=False)
                pe.matmul(bank(2), lw[:, 3, :], lora[:, 3, :], start=False, stop=True).then_inc(lw_mm, 1)
                if i is not None:
                    unit_waits(i, 0)
                    unit(pe, tile_unit(i, 0), 0, bank(6))
                pe.wait_ge(kk_ready, j + 1)
                pe.matmul(bank(3), headones[:, :], t2, start=True, stop=True).then_inc(kksum_ready, 1)
                if i is not None:
                    unit_waits(i, 1)
                    unit(pe, tile_unit(i, 1), 1, bank(7), 0, KT // 2)
                pe.wait_ge(bprod_ready, j + 1)
                pe.matmul(bank(4), headones[:, :], t2, start=True, stop=True).then_inc(bsum_ready, 1)
                if i is not None:
                    unit(pe, tile_unit(i, 1), 1, bank(7), KT // 2, KT)

            def pe_b(j, fill):
                pe.wait_ge(prep_done, j + 1)
                for n, (src, dst) in enumerate(((v_, 0), (Bt[:, :], 1), (Kt[:, :], 2), (AR[:, 0, :], 3))):
                    for tt in range(TT):
                        last = pe.transpose(bank(dst)[:, tt * P:tt * P + P], src[:, tt * P:tt * P + P], ident[:, :])
                    last.then_inc(tr_ready, 1)
                fill(F_TR)
                hs = [slice(CH * h, CH * h + CH) for h in range(2)]
                for m in range(8):
                    h, tt = divmod(m, TT)
                    t = slice(P * tt, P * tt + P)
                    if m >= 2:
                        pe.wait_ge(intra_saved, 8 * j + m - 1)
                    for n, lhs in enumerate((Bt, Kt)):
                        last = pe.matmul(bank(4 + m % 2)[:, 256 * n:256 * n + 256].rearrange("p (a t) -> p a t", a=2),
                                         lhs[hs[h], t], AR[hs[h], :, t], start=True, stop=True)
                    last.then_inc(intra_ready, 1)
                    if m % 2:
                        fill(F_INTRA)
                pe.wait_ge(xt0_ready, j + 1)
                pe.wait_ge(tr_savedA, 2 * j + 2)
                for m in range(8):
                    last = pe.transpose(bank(m // 4)[:, (m % 4) * P:(m % 4) * P + P], XT[:, m, :], ident[:, :])
                    if m % 4 == 3:
                        last.then_inc(x0_ready, 1)
                fill(F_X0)
                pe.wait_ge(tr_savedD, 2 * j + 2)
                pe.wait_ge(intra_saved, 8 * j + 8)
                part = lambda b, m: bank(b + m // 4)[:, (m % 4) * P:(m % 4) * P + P]
                for n in range(1, len(LEVELS)):
                    lv = 5 * j + n - 1
                    pe.wait_ge(mb_ready, lv + 1)
                    if n == 1:
                        pe.wait_ge(x0_saved, 2 * j + 2)
                    else:
                        pe.wait_ge(x_saved, 2 * (4 * j + n - 1))
                    for m in range(8):
                        last = pe.matmul(part(0, m), Mb[:, m, :], X[:, m, :], start=True, stop=True)
                        if m % 4 == 3:
                            last.then_inc(z_ready, 1)
                    fill(F_LEVEL)
                    pe.wait_ge(z_saved, 2 * lv + 2)
                    if n > 1:
                        pe.wait_ge(xt_saved, 2 * lv)
                    if n < len(LEVELS) - 1:
                        for m in range(8):
                            last = pe.matmul(part(2, m), XT[:, m, :], Z[:, m, :], start=True, stop=True)
                            if m % 4 == 3:
                                last.then_inc(xx_ready, 1)
                    for m in range(8):
                        last = pe.matmul(part(4, m), Z[:, m, :], XT[:, m, :], start=True, stop=True)
                        if m % 4 == 3:
                            last.then_inc(xt_ready, 1)
                    fill(F_LEVEL)
                pe.wait_ge(xt_saved, 2 * (5 * j + 5))
                for m in range(8):
                    h, tt = divmod(m, TT)
                    last = pe.matmul(bank(0)[hs[h], P * tt:P * tt + P], An[:, tt, hs[h]], XT[:, m, :], start=True, stop=True)
                last.then_inc(wt_ready, 1)
                for m in range(8):
                    h, tt = divmod(m, TT)
                    last = pe.matmul(part(4, m), M4[:, m, 2, :], Vn[:, tt, :], start=True, stop=True)
                last.then_inc(akv_ready, 1)
                fill(F_W)
                pe.wait_ge(akv_saved, 2 * j + 2)
                for m in range(8):
                    h, tt = divmod(m, TT)
                    last = pe.matmul(part(2, m), XT[:, m, :], AKVf[:, CH * m:CH * m + P], start=True, stop=True)
                last.then_inc(g_ready, 1)
                fill(F_G)
                pe.wait_ge(wt_saved, j + 1)
                pe.wait_ge(g_saved, j + 1)
                for c in range(NCH):
                    tt, q = divmod(c, 2)
                    pe.matmul(bank(3)[hs[q], 0:P], WT[:, CH * c:CH * c + CH], Sh[:, c, :], start=True, stop=True).then_inc(u_ready, 1)
                    fill(F_U)
                    pe.wait_ge(u_saved, NCH * j + c + 1)
                    pe.matmul(bank(4)[:, 0:P], Kn[hs[q], tt, :], Vn[hs[q], tt, :], start=True, stop=False)
                    pe.matmul(bank(4)[:, 0:P], Bn[hs[q], tt, :], Un[hs[q], tt, :, :].rearrange("p h c -> p (h c)"),
                              start=False, stop=True).then_inc(s_ready, 1)
                    fill(F_S)
                    pe.wait_ge(s_saved, NCH * j + c + 1)
                for c in range(NCH):
                    pe.matmul(bank(0)[:, CH * c:CH * c + CH], Sh[:, c, :], AR[:, 1, CH * c:CH * c + CH],
                              start=c == 0, stop=False, skip_group_check=True)
                for h in range(2):
                    for tt in range(TT):
                        dst = bank(0)[hs[h], P * tt:P * tt + P]
                        pe.matmul(dst, Un[:, tt, h, :], M4[:, TT * h + tt, 1, :], start=False, stop=False, skip_group_check=True)
                        last = pe.matmul(dst, Vn[:, tt, hs[h]], M4[:, TT * h + tt, 3, :], start=False, stop=True, skip_group_check=True)
                last.then_inc(y_ready, 1)
                pe.wait_ge(y_saved, j + 1)
                pe.matmul(bank(1), headones[:, :], ysb[:, :], start=True, stop=True).then_inc(mean_ready, 1)
                pe.wait_ge(ysq_ready, j + 1)
                pe.matmul(bank(5), headones[:, :], ysq[:, :], start=True, stop=True).then_inc(yvar_ready, 1)

            for c in range(4):
                unit_waits(0, c)
                unit(pe, tile_unit(0, c), c % 2, bank(6 + c % 2))
            pe.wait_ge(consts, 2)
            with pe.Fori(1, RJ) as i:
                pe_prep(i - 1, i)
                pe_b(i - 1, Filler(pe, tile_unit(i, 2), 6, lambda c: unit_waits(i, 2 + c)))
            pe_prep(RJ - 1, None)
            pe_b(RJ - 1, Filler(pe, U_MLSTM - N_SIDE, N_SIDE, lambda c: pe.wait_ge(side_saved, 5 * RJ - 4 + max(c - 1, 0))))

            pe.wait_ge(rows_ready, 1)
            for tt in range(TT):
                last = pe.transpose(bank(4)[:, MH * tt:MH * tt + MH], rows[:, 3, tt * P:tt * P + P], ident[0:MH, 0:MH])
            last.then_inc(rc_ready, 1)
            pe.wait_ge(nm_ready, 1)
            for h in range(MH):
                for c, src in enumerate((5, 4)):
                    if h:
                        pe.wait_ge(rb_saved, 2 * h + c - 1)
                    pe.matmul(bank(2 + c), sel[:, h, :], rows[:, src, :], start=True, stop=True).then_inc(rb_ready, 1)
            pe.wait_ge(rb_saved, 2 * MH)

            def pe_m(h, first=False):
                n = U_MLSTM + 6 * h
                for c in range(4):
                    if c >= 2:
                        pe.wait_ge(pc_saved, 4 * h + c - 1)
                    elif not first:
                        pe.wait_ge(pc_saved, 4 * h)
                    else:
                        pe.wait_ge(side_saved, 5 * RJ)
                    unit(pe, n + c, c % 2, bank(6 + c % 2))
                    if not first and c == 0:
                        pe_scores_m(h - 1)
                    if not first and c == 1:
                        pe_heads(h - 1)
                if not first:
                    pe.wait_ge(v_saved, 2 * h)
                for c in range(2):
                    pe.wait_ge(w_lo, n + 5 + c)
                    for tt in range(TT):
                        dst = bank(tt // 2)[:, 256 * (tt % 2):256 * (tt % 2) + 256]
                        for k in range(8):
                            lh, ll = xh[:, 8 * c + k, P * tt:P * tt + P], xl[:, 8 * c + k, P * tt:P * tt + P]
                            w_h, w_l = wh[c][:, 256 * k:256 * k + 256], wl[c][:, 256 * k:256 * k + 256]
                            new = c == 0 and k == 0 and tt % 2 == 0
                            pe.matmul(dst, lh, w_h, start=new, stop=False, skip_group_check=True)
                            pe.matmul(dst, lh, w_l, start=False, stop=False, skip_group_check=True)
                            last = pe.matmul(dst, ll, w_h, start=False, stop=c == 1 and k == 7, skip_group_check=True)
                    last.then_inc(w_used, 1)

            SC = [(2, 0), (3, 0), (4, 0), (3, 384)]

            def pe_scores_m(h):
                pe.wait_ge(qk_ready, 4 * h + 4)
                for i in range(TT):
                    lo = P * i
                    b, at = SC[i]
                    for c in range(2):
                        last = pe.matmul(bank(b)[:, at:at + T - lo], QK[:, 2 + c, lo:lo + P], QK[:, c, lo:T], start=c == 0, stop=c == 1)
                    last.then_inc(sc_ready, 1)

            def pe_heads(h):
                pe.wait_ge(v_saved, 2 * h + 2)
                pe.wait_ge(sd_ready, TT * h + TT)
                for b, lhs in ((5, lambda i: Vm[:, i, 0:P]), (2, lambda i: Vm[:, i, P:2 * P]), (3, lambda i: ones[:, :])):
                    for i in range(TT):
                        last = pe.matmul(bank(b)[:, P * i:T], lhs(i), SD[:, i, P * i:T], start=i == 0, stop=i == TT - 1)
                last.then_inc(hm_ready, 1)

            pe_m(0, first=True)
            with pe.Fori(1, MH) as h:
                pe_m(h)
            pe_scores_m(MH - 1)
            pe_heads(MH - 1)

            pe.wait_ge(ym_ready, MH)
            pe.wait_ge(yl_ready, 4)

            def pe_mix(d, dd, first=False):
                if not first:
                    pe.wait_ge(mix_ready, 2 * d + dd - 1)
                pe.wait_ge(w_lo, U_MIX + 2 * d + dd + 1)
                for c in range(2):
                    for k in range(8):
                        last = products(pe, bank(2 * dd + c), dd, 8 * c + k, P, yh, yl, 8 * c + k, k == 0, k == 7)
                last.then_inc(w_used, 1)

            for dd in range(2):
                pe_mix(0, dd, first=True)
            with pe.Fori(1, KT // 2) as d:
                for dd in range(2):
                    pe_mix(d, dd)
            pe.wait_ge(mix_ready, KT)
            for c in range(2):
                pe.wait_ge(w_lo, U_OUT + c + 1)
                for k in range(KT):
                    pe.wait_ge(ml_ready, k + 1)
                    last = products(pe, bank(c), c, k, P, xh, xl, k, k == 0, k == KT - 1)
                last.then_inc(w_used, 1)
            with pe.Fori(1, KT // 2) as d:
                for c in range(2):
                    pe.wait_ge(h_ready, 2 * d + c - 1)
                    unit(pe, U_OUT + 2 * d + c, c, bank(c))
            norm_pe(sq2)
            pe.wait_ge(keys_in, 16)

            def key_products(h, c):
                pe.wait_ge(q_saved, 2 * h + c + 1)
                for tt in range(TT):
                    last = pe.matmul(bank(2 + c)[:, P * tt:P * tt + P], qsb[:, c, P * tt:P * tt + P], keys[:, c, :], start=True, stop=True)
                last.then_inc(key_scores, 1)

            for c in range(2):
                first_unit(U_QUERY + c, c, bank(c), 1)

            def ahead(e, s, n):
                if not (isinstance(e, int) and e < 2):
                    pe.wait_ge(pre_ready, e - 1)
                unit(pe, n, s, bank(4 + s))

            for c in range(2):
                key_products(0, c)
                ahead(c, c, U_QUERY + 2 + c)
            with pe.Fori(1, HEADS) as h:
                for c in range(2):
                    unit(pe, U_QUERY + 4 * h + c, c, bank(c))
                for c in range(2):
                    pe.wait_ge(ssb_saved, 2 * h + c - 1)
                    key_products(h, c)
                    ahead(2 * h + c, c, U_QUERY + 4 * h + 2 + c)
            for e in range(2 * HEADS, 2 * AHEAD):
                ahead(e, e % 2, U_TAIL + e - 2 * HEADS)
            pe.wait_ge(routed, HEADS)
            pe.wait_ge(pre_ready, 2 * AHEAD)
            for m in range(3):
                for tt in range(TT):
                    last = pe.transpose(bank(4 + m)[:, P * tt:P * tt + P], EG[:, m, tt, :], ident[:, :])
                last.then_inc(egt_ready, 1)

            def dense(i, first=False):
                for c in range(4):
                    if not first:
                        pe.wait_ge(dense_saved, 4 * i + c - 3)
                    for u in range(4):
                        s = (4 * c + u) % OH
                        pe.wait_ge(oh_ready, 16 * i + 4 * c + u + 1)
                        last = pe.matmul(bank(c)[:, P * u:P * u + P], oh[s][0][:, :], oh[s][1][:, :], start=True, stop=True)
                        last.then_inc(oh_used, 1)

            dense(0, first=True)
            with pe.Fori(1, T // 16) as i:
                dense(i)

            def pe_scores(g, n0, first=False):
                for e in range(2):
                    if not first:
                        pe.wait_ge(gelu_ready, 2 * (g - AHEAD) + e - 1)
                    unit(pe, n0 + e, e, bank(e))

            def pe_values(g, s, n0, first=False):
                pe.wait_ge(gal_ready, 2 * g + 2)
                for half in range(2):
                    pe.wait_ge(w_lo, n0 + half + 1)
                    for dd in range(8):
                        d = 8 * half + dd
                        if not (first and d < 4):
                            pe.wait_ge(out_added, KT * g + d - 3)
                        for e in range(2):
                            last = products(pe, bank(2 + d % 4), half, 8 * e + dd, P, gah[s], gal[s], e, e == 0, e == 1)
                        if dd == 7:
                            last.then_inc(w_used, 1)
                        else:
                            last.then_inc(out_ready, 1)

            pe.wait_ge(dense_saved, T // 4)
            pe_values(0, 0, U_PEER, first=True)
            with pe.Fori(1, AHEAD // 2) as i:
                for s in range(2):
                    g = 2 * i + s
                    pe_values(g - 1, (s + 1) % 2, U_PEER + 2 * (g - 1))
            for s in range(2):
                pe_scores(AHEAD + s, U_SCORED + 4 * s, first=s == 0)
                pe_values(AHEAD + s - 1, (s + 1) % 2, U_SCORED + 4 * s + 2)
            with pe.Fori(AHEAD // 2 + 1, GROUPS // 2) as i:
                for s in range(2):
                    g = 2 * i + s
                    pe_scores(g, U_SCORED + 4 * (g - AHEAD))
                    pe_values(g - 1, (s + 1) % 2, U_SCORED + 4 * (g - AHEAD) + 2)
            pe_values(GROUPS - 1, 1, N_UNITS - 2)
            norm_pe(sq3)


STEPS_RWKV, STEPS_MLSTM, STEPS_ROUTE = 38, 21, 93


_INS = ["stream", "lora_w", "params", "x_t", "keys_t"]


def layout(i):
    import numpy as np
    a = {k: np.asarray(v) for k, v in i.items()}
    w_in = a["w_in"][0]
    stream = np.zeros((N_UNITS, P, 2048), np.float32)
    tile = lambda w: w.reshape(-1, P, P).transpose(1, 0, 2).reshape(P, -1)
    RB = 4 * 1024 + 2 * MH
    GBASE = RB + 3 * 1024 + 96 + 96 + 256
    pad = np.zeros((D, 28), np.float32)
    for n in range(2):
        low = w_in[:, RB + 3072 + 96 * n:RB + 3072 + 96 * n + 96]
        stream[n] = tile(np.concatenate([low, w_in[:, 4096 + MH * n:4096 + MH * n + MH], pad], 1))
        stream[2 + n] = tile(w_in[:, RB + 3264 + P * n:RB + 3264 + P * n + P])
    for j in range(RJ):
        at = U_RWKV + max(8 * j - 4, 0)
        for c in range(3):
            stream[at + c] = tile(w_in[:, RB + 1024 * c + P * j:RB + 1024 * c + P * j + P])
        stream[at + 3] = tile(w_in[:, 3072 + P * j:3072 + P * j + P])
        for c in range(N_SIDE):
            q = N_SIDE * j + c
            stream[min(U_RWKV + 8 * (j + 1), U_MLSTM - N_SIDE) + c] = tile(w_in[:, GBASE + P * q:GBASE + P * q + P])
    for h in range(MH):
        for c in range(4):
            at = 1024 * (c // 2) + 256 * h + P * (c % 2)
            stream[U_MLSTM + 6 * h + c] = tile(w_in[:, at:at + P])
        for c in range(2):
            v = w_in[1024 * c:1024 * c + 1024, 2048 + 256 * h:2048 + 256 * h + 256]
            stream[U_MLSTM + 6 * h + 4 + c] = v.reshape(8, P, 256).transpose(1, 0, 2).reshape(P, 2048)
    for d in range(KT):
        cut = slice(P * d, P * d + P)
        stream[U_MIX + d] = tile(np.concatenate([a["proj_mlstm"][0][:, cut], a["proj_rwkv"][0][:, cut]], 0))
        stream[U_OUT + d] = tile(a["w_out"][0][:, cut])
        stream[U_QUERY + 4 * (d // 2) + d % 2] = tile(a["peer_w_query"][0][:, cut])
    u = a["peer_u"][0].reshape(NKEYS, NKEYS, KT, P).transpose(0, 3, 2, 1).reshape(NKEYS, P, 2048)
    v = a["peer_v"][0].reshape(GROUPS, 2, NKEYS, 2, 1024).transpose(0, 3, 2, 1, 4).reshape(GROUPS, 2, P, 2048)
    for g in range(GROUPS):
        at = U_QUERY + 4 * g + 2 if g < HEADS else U_TAIL + 2 * (g - HEADS) if g < AHEAD else U_SCORED + 4 * (g - AHEAD)
        stream[at:at + 2] = u[2 * g:2 * g + 2]
        at = U_PEER + 2 * g if g < AHEAD - 1 else U_SCORED + 4 * (g - AHEAD + 1) + 2 if g < GROUPS - 1 else N_UNITS - 2
        stream[at:at + 2] = v[g]
    lora = np.zeros((4, P, 1024), np.float32)
    lora[0, :96], lora[1, :96] = a["rwkv_w2"][0], a["rwkv_a2"][0]
    lora[2:4] = a["rwkv_g2"][0].reshape(2, P, 1024)
    lora_w = np.ascontiguousarray(lora.reshape(4, P, RJ, P).transpose(2, 1, 0, 3))
    par = np.zeros((P, N_PAR), np.float32)
    mu = a["rwkv_mu"][0]
    per = [mu[0:1024], mu[1024:2048], mu[2048:3072], a["rwkv_w0"][0], a["rwkv_a0"][0], a["rwkv_k_k"][0],
           a["rwkv_k_a"][0], a["rwkv_r_k"][0].reshape(-1), a["rwkv_ln_w"][0], a["rwkv_ln_b"][0]]
    par[:, 0:C_LMU] = np.stack(per).reshape(N_RP, RJ, P).transpose(2, 1, 0).reshape(P, -1)
    par[:96, C_LMU], par[:96, C_LMU + 1] = mu[3072:3168], mu[3168:3264]
    par[:, C_LMU + 2:C_LMU + 4] = mu[3264:3520].reshape(2, P).T
    par[:MH, C_BI], par[:MH, C_BI + 1] = a["mlstm_b_i"][0], a["mlstm_b_f"][0]
    par[:, C_CONV:C_GAIN] = a["mlstm_conv"][0].reshape(4, 16, P).transpose(2, 1, 0).reshape(P, -1)
    gains = np.stack([a["norm_mix_gain"][0], a["norm_ffn_gain"][0], a["norm_final_gain"]])
    par[:, C_GAIN:] = gains.reshape(3, KT, P).transpose(2, 0, 1).reshape(P, -1)
    x_t = np.ascontiguousarray(a["x"][0].T.reshape(KT, P, T))
    keys_t = np.ascontiguousarray(a["peer_sub_keys"][0].transpose(2, 0, 1))
    return {"stream": stream, "lora_w": lora_w, "params": par, "x_t": x_t, "keys_t": keys_t}


def kernel(**inputs):
    import numpy as np
    import concourse.bacc as bacc
    from concourse.bass_utils import run_bass_kernel_spmd

    nc = bacc.Bacc("TRN2", target_bir_lowering=False, num_devices=1)
    arrays = layout(inputs)
    args = [nc.dram_tensor(k, arrays[k].shape, F32, kind="ExternalInput").ap() for k in _INS]
    out = nc.dram_tensor("out", (KT, P, T), F32, kind="ExternalOutput").ap()
    build(nc, *args, out)
    r = run_bass_kernel_spmd(nc, [arrays], core_ids=[0])
    y = r.results[0]["out"]
    return np.ascontiguousarray(y.reshape(D, T).T).reshape(1, T, D)
```

```python
from contextlib import ExitStack

import concourse.bass as bass
from concourse import mybir
from concourse.alu_op_type import AluOpType as ALU

F32 = mybir.dt.float32
F32R = mybir.dt.float32r
BF16 = mybir.dt.bfloat16
U32 = mybir.dt.uint32
ACT = mybir.ActivationFunctionType
AX = mybir.AxisListType

P = 128
T = 512
TT = T // P
D = 2048
KT = D // P
CH = 64
NCH = T // CH
RJ = 1024 // P
MH = 4
HEADS, TOPK, NKEYS = 8, 16, 128
DECAY = float(2.718281828459045 ** -0.5)
RMS_EPS, GN_EPS, L2_EPS = 1e-6, 64e-5, 1e-12
LEVELS = [1, 2, 4, 8, 16, 32]

N_LORA = 4
N_SIDE = 4
U_RWKV = N_LORA
U_MLSTM = U_RWKV + (4 + N_SIDE) * RJ
U_MIX = U_MLSTM + 6 * MH
U_OUT = U_MIX + KT
U_QUERY = U_OUT + KT
GROUPS = NKEYS // 2
AHEAD = HEADS + 4
U_TAIL = U_QUERY + 4 * HEADS
N_TAIL = 6
U_PEER = U_TAIL + 2 * (AHEAD - HEADS)
U_SCORED = U_PEER + 2 * (AHEAD - 1)
N_UNITS = U_PEER + 2 * GROUPS + 2 * (GROUPS - AHEAD)

F_PREP, F_INTRA, F_XT, F_X0, F_Z, F_X, F_W, F_G, F_U, F_S, F_YM, F_Y = 10, 1, 6, 2, 4, 3, 2, 2, 2, 2, 2, 2

C_RP, N_RP = 0, 10
C_LMU = C_RP + RJ * N_RP
C_BI = C_LMU + N_LORA
C_CONV = C_BI + 2
C_GAIN = C_CONV + 16 * 4
N_PAR = C_GAIN + 3 * KT


class Steps:

    def __init__(self, eng, sem):
        self.eng, self.sem, self.base, self.n = eng, sem, 0, 0

    def __call__(self, ins):
        ins.then_inc(self.sem, 1)
        self.n += 1
        self.eng.wait_ge(self.sem, self.base + self.n)

    def enter(self, i, first, per):
        self.kept = (self.base, self.n, per)
        self.base, self.n = per * (i - first) + (self.base + self.n), 0

    def leave(self, times):
        base, n, per = self.kept
        assert self.n == per, f"steps in the loop's body: {self.n}"
        self.base, self.n = base, n + per * times


def own(eng, ins, sem, value):
    ins.then_inc(sem, 1)
    eng.wait_ge(sem, value)


def build(nc, stream, lora_w, params, x_t, keys_t, out_t):
    dram = lambda name, shape: nc.dram_tensor(name, shape, F32, kind="Internal").ap()
    yr_d = dram("yr_scratch", (RJ, P, T))
    ym_d = dram("ym_scratch", (2 * MH, P, T))
    og_d = dram("ogate_scratch", (2 * MH, P, T))
    if_d = dram("if_scratch", (2, MH, T))
    sg_d = dram("mergegate_scratch", (2 * KT, P, T))
    act_d = dram("gelu_scratch", (2 * AHEAD, P, T))
    GB = 16
    GT = T // GB
    gate_d = dram("gates_scratch", (GB, P, NKEYS, GT))

    ctx = ExitStack()
    with ctx:
        stack = [ctx]
        sb = lambda name, shape, dt=F32: stack[-1].enter_context(nc.sbuf_tensor(name, shape, dt))
        sem = lambda name: ctx.enter_context(nc.semaphore(name))
        ps = ctx.enter_context(nc.psum_tensor("ps", [P, 8, 512], F32))
        bank = lambda b: ps[:, b, :]

        xh = sb("xh", [P, KT, T], F32R)
        xl = sb("xl", [P, KT, T], F32R)
        raw = [sb(f"raw{s}", [P, 2048]) for s in range(2)]
        wh = [sb(f"wh{s}", [P, 2048], F32R) for s in range(2)]
        wl = [sb(f"wl{s}", [P, 2048], F32R) for s in range(2)]
        par = sb("par", [P, N_PAR])
        ident = sb("ident", [P, P])
        ones = sb("ones", [P, P])
        headones = sb("headones", [P, P])
        tri = sb("tri", [P, P], BF16)
        cst = sb("cst", [P, 2])
        iota16 = sb("iota16", [P, TOPK]); iota128 = sb("iota128", [P, P])

        def phase():
            if len(stack) > 1:
                stack.pop().close()
            stack.append(ExitStack())

        phase()
        H1 = sb("h_in", [P, KT, T])
        sq1 = sb("sq1", [P, 2, T]); nt1 = sb("nt1", [P, 2, T]); rstd1 = sb("rstd1", [P, T])
        phase()
        lora = sb("lora", [P, N_LORA, T])
        lw = sb("lw", [P, N_LORA, P])
        pin = [sb(f"pin{c}", [P, T + 1]) for c in range(3)]
        plo = pin[0]
        g_sb = sb("g_sb", [P, T]); bonus = sb("bonus", [P, T])
        AR = sb("AR", [P, 2, T]); Bt = sb("Bt", [P, T]); Kt = sb("Kt", [P, T])
        Vn = sb("Vn", [P, TT, P]); Bn = sb("Bn", [P, TT, P]); Kn = sb("Kn", [P, TT, P]); An = sb("An", [P, TT, P])
        WT = sb("WT", [P, T]); Gn = sb("Gn", [P, 2, TT, CH]); Un = sb("Un", [P, TT, 2, CH])
        Sh = sb("Sh", [P, NCH + 1, P]); SE = sb("SE", [P, P]); EL = sb("EL", [P, NCH])
        ysb = sb("ysb", [P, T]); yc = sb("yc", [P, T]); ysq = sb("ysq", [P, T])
        sgb = sb("sgb", [P, 2, T])
        mask4 = sb("mask4", [P, 4, P], BF16)
        lev = sb("lev", [P, len(LEVELS), P], BF16)
        reset = sb("reset", [P, T], BF16)
        over = sb("over", [P, 16, T])
        r_, k_, v_, sg, cs, E0, E1, E2, a_, kk, t1, t2 = (over[:, n, :] for n in range(12))
        M4 = over[:, 0:8, :].rearrange("p n (a t) -> p n a t", a=4)
        X = over[:, 8:10, :].rearrange("p n (a t) -> p (n a) t", a=4)
        XT = over[:, 10:12, :].rearrange("p n (a t) -> p (n a) t", a=4)
        Z = over[:, 12:14, :].rearrange("p n (a t) -> p (n a) t", a=4)
        Mb = over[:, 14:16, :].rearrange("p n (a t) -> p (n a) t", a=4)
        AKVf = over[:, 12:14, :].rearrange("p n t -> p (n t)")
        AKV = AKVf[:, 0:T].rearrange("p (h n c) -> p h n c", h=2, n=TT)
        phase()
        sb("mlstm_gap", [P, 2176])
        rows = sb("rows", [MH, 8, T])
        pc = [sb(f"pc{c}", [P, T + 3]) for c in range(4)]
        cacc = sb("cacc", [P, 2, T])
        sel = sb("sel", [MH, MH, P])
        QK = sb("QK", [P, 4, T])
        Dm = sb("Dm", [P, TT, T])
        Vm = sb("Vm", [P, TT, 256])
        SD = sb("SD", [P, TT, T])
        rcol = sb("rcol", [P, TT, MH])
        og = sb("og", [P, 2, T])
        RNb = sb("RNb", [P, MH, 2, T])
        rec = sb("rec", [P, T]); ymo = sb("ymo", [P, 2, T])
        phase()
        yrraw = [sb(f"yrraw{s}", [P, T]) for s in range(2)]
        yh_r = sb("yh_r", [P, RJ, T], F32R); yl_r = sb("yl_r", [P, RJ, T], F32R)
        yh_m = sb("yh_m", [P, 2 * MH, T], F32R); yl_m = sb("yl_m", [P, 2 * MH, T], F32R)
        ymraw = sb("ymraw", [P, MH - 1, 2, T])
        sgm = sb("sgm", [P, 2, 2, T]); mxo = sb("mxo", [P, 2, T])
        phase()
        H = sb("H", [P, KT, T])
        preb = sb("preb", [P, 2, T])

        def subphase():
            stack.pop().close()
            stack.append(ExitStack())

        stack.append(ExitStack())
        sum2 = sb("sum2", [P, T]); sq2 = sb("sq2", [P, T]); nt2 = sb("nt2", [P, 2, T]); rstd2 = sb("rstd2", [P, T])
        subphase()
        EGT = sb("EGT", [P, 3, T])
        stack.append(ExitStack())
        EG = sb("EG", [P, 3, TT, P])
        keys = sb("keys", [P, 2, P])
        qsb = sb("qsb", [P, 2, T])
        ssb = sb("ssb", [P, 2, TT, P]); srep = sb("srep", [P, P])
        v16 = sb("v16", [P, 2, TT, TOPK]); i16 = sb("i16", [P, 2, TT, TOPK], U32); if16 = sb("if16", [P, 2, TT, TOPK])
        cand = sb("cand", [P, 256]); crep = sb("crep", [P, 256])
        best = sb("best", [P, TT, TOPK]); ci = sb("ci", [P, TT, TOPK], U32)
        chi = sb("chi", [P, 2, TT, TOPK], U32); chf = sb("chf", [P, 2, TT, TOPK])
        eq = sb("eq", [P, TOPK, TOPK])
        ex = sb("ex", [P, TT, TOPK]); sm = sb("sm", [P, 2, TT])
        subphase()
        OH = 16
        oh2 = sb("oh2", [P, OH, P]); oh1 = sb("oh1", [P, OH, P])
        stage = [sb(f"stage{s}", [P, NKEYS, GT]) for s in range(2)]
        stack.pop().close()
        subphase()
        gt = sb("gt", [P, 2, 2, T]); act_ = sb("act_", [P, 2, 2, T])
        gah = [sb(f"gah{s}", [P, 2, T], F32R) for s in range(2)]
        gal = [sb(f"gal{s}", [P, 2, T], F32R) for s in range(2)]
        sq3 = sb("sq3", [P, 2, T]); sum3 = sb("sum3", [P, T]); rstd3 = sb("rstd3", [P, T])
        stack.pop().close()
        stack.pop().close()

        w_loaded = [sem("w_loaded0"), sem("w_loaded1")]
        w_hi, w_lo, w_used = sem("w_hi"), sem("w_lo"), sem("w_used")
        par_in, x_in, keys_in = sem("par_in"), [sem(f"x_in{c}") for c in range(4)], sem("keys_in")
        consts = sem("consts")
        passed = sem("passed")
        pool_step, dve_step, act_step = sem("pool_step"), sem("dve_step"), sem("act_step")
        sq_ready, sq_used, sq_summed, sum_ready, var_sum = (sem(n) for n in ("sq_ready", "sq_used", "sq_summed", "sum_ready", "var_sum"))
        var_ready, std_ready, nt_ready, nh_ready, nl_ready = (sem(n) for n in ("var_ready", "std_ready", "nt_ready", "nh_ready", "nl_ready"))
        lora_p, lora_s, lora_ready = sem("lora_p"), sem("lora_s"), sem("lora_ready")
        lw_in, lw_mm, lw_taken = sem("lw_in"), sem("lw_mm"), sem("lw_taken")
        pin_saved, shifted = sem("pin_saved"), sem("shifted")
        cs_ready, exps_ready, kk_ready, kksum_ready, kknorm_ready = (sem(n) for n in ("cs_ready", "exps_ready", "kk_ready", "kksum_ready", "kknorm_ready"))
        bprod_ready, bsum_ready, prep_done = sem("bprod_ready"), sem("bsum_ready"), sem("prep_done")
        tr_ready, tr_savedA, tr_savedD = sem("tr_ready"), sem("tr_savedA"), sem("tr_savedD")
        intra_ready, intra_saved = sem("intra_ready"), sem("intra_saved")
        xt0_ready, x0_ready, x0_saved, mb_ready = sem("xt0_ready"), sem("x0_ready"), sem("x0_saved"), sem("mb_ready")
        z_ready, z_saved, xx_ready, xt_ready = sem("z_ready"), sem("z_saved"), sem("xx_ready"), sem("xt_ready")
        x_saved, xt_saved = sem("x_saved"), sem("xt_saved")
        wt_ready, wt_saved, akv_ready, akv_saved, g_ready, g_saved = (sem(n) for n in ("wt_ready", "wt_saved", "akv_ready", "akv_saved", "g_ready", "g_saved"))
        u_ready, u_saved, s_ready, s_saved = sem("u_ready"), sem("u_saved"), sem("s_ready"), sem("s_saved")
        y_ready, y_saved, mean_ready, ysq_ready, yvar_ready, ystd_ready, yo_ready = (sem(n) for n in ("y_ready", "y_saved", "mean_ready", "ysq_ready", "yvar_ready", "ystd_ready", "yo_ready"))
        side_saved, yr_stored, if_stored = sem("side_saved"), sem("yr_stored"), sem("if_stored")
        sg_stored = [sem("sg_stored0"), sem("sg_stored1")]
        rows_in, rows_ready, rc_ready, rc_saved, rb_ready, rb_saved = sem("rows_in"), sem("rows_ready"), sem("rc_ready"), sem("rc_saved"), sem("rb_ready"), sem("rb_saved")
        lf_e, lf_ln, nm_ready = sem("lf_e"), sem("lf_ln"), sem("nm_ready")
        pc_saved, conv_ready, qk_ready, v_saved = sem("pc_saved"), sem("conv_ready"), sem("qk_ready"), sem("v_saved")
        arg_ready, dm_ready, sc_ready, sd_ready = sem("arg_ready"), sem("dm_ready"), sem("sc_ready"), sem("sd_ready")
        den_ready, hm_ready, ym_ready, ym_stored, og_in = sem("den_ready"), sem("hm_ready"), sem("ym_ready"), sem("ym_stored"), sem("og_in")
        yr_in, yrh_ready, yrl_ready = [sem("yr_in0"), sem("yr_in1")], sem("yrh_ready"), sem("yrl_ready")
        ym_in, ymh_ready, yml_ready = [sem(f"ym_in{h}") for h in range(MH - 1)], sem("ymh_ready"), sem("yml_ready")
        sg_in, mix_ready = [sem("sg_in0"), sem("sg_in1")], sem("mix_ready")
        mh_ready, ml_ready, h_in, h_ready = sem("mh_ready"), sem("ml_ready"), sem("h_in"), sem("h_ready")
        pre_ready, pre_in = sem("pre_ready"), [sem("pre_in0"), sem("pre_in1")]
        pre_stored = [sem("pre_stored0"), sem("pre_stored1")]
        q_saved, key_scores, ssb_saved, sel_done = sem("q_saved"), sem("key_scores"), sem("ssb_saved"), sem("sel_done")
        best_ready, ex_ready, routed, egt_ready, egt_saved = sem("best_ready"), sem("ex_ready"), sem("routed"), sem("egt_ready"), sem("egt_saved")
        oh_ready, gated_ready, dense_saved, oh_used = sem("oh_ready"), sem("gated_ready"), sem("dense_saved"), sem("oh_used")
        gates_stored = [sem("gates_stored0"), sem("gates_stored1")]
        gt_in, gelu_ready, ga_ready, gah_ready, gal_ready = [sem("gt_in0"), sem("gt_in1")], sem("gelu_ready"), sem("ga_ready"), sem("gah_ready"), sem("gal_ready")
        out_ready, out_added, last_ready, out_stored = sem("out_ready"), sem("out_added"), sem("last_ready"), sem("out_stored")

        rp = lambda j, c: par[:, bass.ds(j * N_RP + c, 1)]

        def load_unit(sp, n, s, first=False):
            if not first:
                sp.wait_ge(w_lo, n - 1)
            sp.dma_start(raw[s][:, :], stream[bass.ds(n, 1)].rearrange("a p n -> p (a n)")).then_inc(w_loaded[s], 16)

        def split_hi(act, n, s, first=False):
            act.wait_ge(w_loaded[s], 8 * n + 16 - 8 * s)
            if not first:
                act.wait_ge(w_used, n - 1)
            act.activation(wh[s][:, :], raw[s][:, :], ACT.Copy).then_inc(w_hi, 1)

        def split_lo(pool, n, s):
            pool.wait_ge(w_hi, n + 1)
            pool.tensor_tensor(wl[s][:, :], raw[s][:, :], wh[s][:, :].bitcast(F32), ALU.subtract).then_inc(w_lo, 1)

        def products(pe, dst, s, k, n, h, l, kx, start, stop):
            w_h, w_l = wh[s][:, k * P:(k + 1) * P], wl[s][:, k * P:(k + 1) * P]
            pe.matmul(dst, w_h, h[:, kx, :], start=start, stop=False)
            pe.matmul(dst, w_h, l[:, kx, :], start=False, stop=False)
            return pe.matmul(dst, w_l, h[:, kx, :], start=False, stop=stop)

        def unit(pe, n, s, dst, k0=0, k1=KT):
            if k0 == 0:
                pe.wait_ge(w_lo, n + 1)
            for k in range(k0, k1):
                last = products(pe, dst, s, k, P, xh, xl, k, k == 0, k == KT - 1)
            if k1 == KT:
                last.then_inc(w_used, 1)

        class Filler:
            def __init__(self, pe, n, units, waits):
                self.pe, self.n, self.units, self.at, self.waits = pe, n, units, 0, waits

            def __call__(self, m):
                for _ in range(m):
                    c, k = divmod(self.at, KT)
                    if c < self.units:
                        if k == 0:
                            self.waits(c)
                        unit(self.pe, self.n + c, c % 2, bank(6 + c % 2), k, k + 1)
                        self.at += 1

        class Follower:
            def __init__(self, units, keep):
                self.units, self.at, self.keep = units, 0, keep

            def __call__(self, m):
                for _ in range(m):
                    self.at += 1
                    if self.at % KT == 0 and self.at // KT <= self.units:
                        self.keep(self.at // KT - 1)

        def tile_unit(i, c):
            return U_RWKV + c if isinstance(i, int) and i == 0 else U_RWKV + 8 * i - 4 + c

        block = ctx.enter_context(nc.Block())

        @block.sync
        def _(sp):
            sp.dma_start(par[:, :], params).then_inc(par_in, 16)
            for c in range(4):
                sp.dma_start(H1[:, 4 * c:4 * c + 4, :], x_t[4 * c:4 * c + 4].rearrange("k p t -> p k t")).then_inc(x_in[c], 16)
            for n in range(2):
                load_unit(sp, n, n, first=True)
            for n in range(2, N_LORA):
                load_unit(sp, n, n % 2)
            sp.wait_ge(nl_ready, KT)
            def load_lora(j):
                sp.dma_start(lw[:, :, :], lora_w[bass.ds(j, 1)].rearrange("a p c n -> p (a c) n")).then_inc(lw_in, 16)

            for c in range(4):
                load_unit(sp, U_RWKV + c, c % 2)
            load_lora(0)
            with sp.Fori(1, RJ) as j:
                for c in range(4 + N_SIDE):
                    load_unit(sp, tile_unit(j, c), c % 2)
                sp.wait_ge(lw_mm, 3 * j)
                load_lora(j)
            for c in range(N_SIDE):
                load_unit(sp, U_MLSTM - N_SIDE + c, c % 2)
            for c in range(4):
                load_unit(sp, U_MLSTM + c, c % 2)
            sp.wait_ge(if_stored, 32)
            sp.wait_ge(yo_ready, RJ)
            for c in range(2):
                sp.dma_start(rows[:, c, :], if_d[c]).then_inc(rows_in, 16)
            sp.wait_ge(yr_stored, 16 * RJ)
            for s, stores in enumerate((2 * RJ, 3 * RJ)):
                sp.wait_ge(sg_stored[s], 16 * (stores + 1))
            for c in range(4, 6):
                load_unit(sp, U_MLSTM + c, c % 2)
            with sp.Fori(1, MH) as h:
                for c in range(6):
                    load_unit(sp, U_MLSTM + 6 * h + c, c % 2)
            def load_merge(d, dd):
                for c in range(2):
                    sp.dma_start(sgm[:, dd, c, :], sg_d[bass.ds(2 * d + dd + KT * c, 1)].rearrange("a p t -> p (a t)")).then_inc(sg_in[dd], 16)

            for dd in range(2):
                load_unit(sp, U_MIX + dd, dd)
            sp.wait_ge(qk_ready, 4 * MH)
            for c in range(RJ):
                if c >= 2:
                    sp.wait_ge(yrl_ready, c - 1)
                sp.dma_start(yrraw[c % 2][:, :], yr_d[c]).then_inc(yr_in[c % 2], 16)
            sp.wait_ge(ym_ready, MH)
            for h in range(MH - 1):
                sp.dma_start(ymraw[:, h, :, :], ym_d[2 * h:2 * h + 2].rearrange("k p t -> p k t")).then_inc(ym_in[h], 16)
            for dd in range(2):
                load_merge(0, dd)
            with sp.Fori(1, KT // 2) as d:
                for dd in range(2):
                    load_unit(sp, U_MIX + 2 * d + dd, dd)
                    sp.wait_ge(mix_ready, 2 * d + dd - 1)
                    load_merge(d, dd)
            with sp.Fori(0, KT // 2) as d:
                for c in range(2):
                    load_unit(sp, U_OUT + 2 * d + c, c)
            with sp.Fori(0, 2 * HEADS) as h:
                for c in range(2):
                    load_unit(sp, U_QUERY + 2 * h + c, c)
            with sp.Fori(0, (N_UNITS - U_TAIL) // 2) as g:
                for c in range(2):
                    load_unit(sp, U_TAIL + 2 * g + c, c)
            for k in range(KT):
                sp.wait_ge(last_ready, k + 1)
                sp.dma_start(out_t[k], H[:, k, :]).then_inc(out_stored, 16)
            sp.wait_ge(out_stored, 16 * KT)

        @block.gpsimd
        def _(pool):
            step = Steps(pool, pool_step)
            sel_ge = lambda v, pattern, cm, base, op=ALU.is_ge: step(pool.affine_select(
                out=v, in_=v, compare_op=op, fill=0.0, base=base, pattern=pattern, channel_multiplier=cm))
            step(pool.memset(ones[:, :], 1.0))
            step(pool.memset(cst[:, 0:1], GN_EPS))
            pool.memset(cst[:, 1:2], 1.0).then_inc(consts, 1)
            for v, n in ((iota16, TOPK), (iota128, P)):
                step(pool.iota(v[:, :], pattern=[[1, n]], base=0, channel_multiplier=0, allow_small_or_imprecise_dtypes=True))
            step(pool.memset(ident[:, :], 0.0))
            step(pool.affine_select(out=ident[:, :], in_=ident[:, :], compare_op=ALU.not_equal, fill=1.0,
                                    base=0, pattern=[[-1, P]], channel_multiplier=1))
            step(pool.memset(headones[:, :], 0.0))
            for q in range(2):
                step(pool.memset(headones[CH * q:CH * q + CH, CH * q:CH * q + CH], 1.0))
            step(pool.memset(tri[:, :], 1.0))
            sel_ge(tri[:, :], [[1, P]], -1, 0)
            for n in range(2):
                split_lo(pool, n, n)
            for a in range(4):
                step(pool.memset(mask4[:, a, :], 0.0))
                for q in range(2):
                    step(pool.memset(mask4[CH * q:CH * q + CH, a, CH * q:CH * q + CH], 1.0))
                sel_ge(mask4[:, a, :], [[1, P]], -1, 0, ALU.is_gt if a % 2 == 0 else ALU.is_ge)
            for n, b in enumerate(LEVELS):
                step(pool.memset(lev[:, n, :], 0.0))
                v = lev[:, n, :].rearrange("p (q h u) -> p q h u", h=2, u=b)[:, :, 1, :]
                step(pool.memset(v, 1.0))
                q = P // (2 * b)
                sel_ge(v, [[-2 * b, q], [0, b]], 1, 0)
                sel_ge(v, [[2 * b, q], [0, b]], -1, b - 1)
            step(pool.memset(reset[:, :], 1.0))
            step(pool.memset(reset[:, :].rearrange("p (c u) -> p c u", u=CH)[:, :, 0:1], 0.0))
            step(pool.memset(Sh[:, :, :], 0.0))
            pool.wait_ge(nl_ready, KT)
            for c in range(2):
                step(pool.memset(pin[c][:, 0:1], 0.0))
            pool.memset(pin[2][:, 0:1], 0.0).then_inc(consts, 1)
            for n in range(2, N_LORA):
                split_lo(pool, n, n % 2)
            with pool.Fori(0, (U_MLSTM - U_RWKV) // 2) as j:
                for c in range(2):
                    split_lo(pool, U_RWKV + 2 * j + c, c)
            for n in range(4):
                split_lo(pool, U_MLSTM + n, n % 2)
            pool.wait_ge(yo_ready, RJ)
            step(pool.memset(sel[:, :, :], 1.0))
            sel_ge(sel[:, :, :], [[-1, MH], [0, P]], 1, 0, ALU.is_ge)
            sel_ge(sel[:, :, :], [[1, MH], [0, P]], -1, 0, ALU.is_ge)
            for c in range(4):
                step(pool.memset(pc[c][:, 0:3], 0.0))
            pool.memset(rows[:, 7, :], 1.0).then_inc(consts, 1)
            with pool.Fori(0, (U_MIX - U_MLSTM - 4) // 2) as h:
                for c in range(2):
                    split_lo(pool, U_MLSTM + 4 + 2 * h + c, c)
            for n in range(2):
                for c in range(4 * n, 4 * n + 4):
                    pool.wait_ge(yrh_ready, c + 1)
                    pool.tensor_tensor(yl_r[:, c, :], yrraw[c % 2][:, :], yh_r[:, c, :].bitcast(F32), ALU.subtract).then_inc(yrl_ready, 1)
                split_lo(pool, U_MIX + n, n)
            with pool.Fori(0, (U_TAIL + N_TAIL - U_MIX) // 2) as h:
                for c in range(2):
                    split_lo(pool, U_MIX + 2 + 2 * h + c, c)

            def gated(i):
                for c in range(OH // 4):
                    pool.wait_ge(oh_ready, OH // 4 * i + c + 1)
                    pool.tensor_tensor(oh1[:, 4 * c:4 * c + 4, :], oh1[:, 4 * c:4 * c + 4, :],
                                       EGT[:, 2, bass.ds(OH * i + 4 * c, 4)].unsqueeze(2).to_broadcast([P, 4, P]),
                                       ALU.mult).then_inc(gated_ready, 1)

            pool.wait_ge(egt_saved, 3)
            with pool.Fori(0, T // OH) as i:
                gated(i)
            with pool.Fori(0, (N_UNITS - U_TAIL - N_TAIL - 2) // 2) as h:
                for c in range(2):
                    split_lo(pool, U_TAIL + N_TAIL + 2 + 2 * h + c, c)

        @block.scalar
        def _(act):
            step = Steps(act, act_step)
            st = {"norms": 0}

            def square(Hs, sq, k):
                act.activation(sq[:, k % 2, :], Hs[:, k, :], ACT.Square).then_inc(sq_ready, 1)

            def norm_act(nt):
                m = st["norms"]; st["norms"] += 1
                act.wait_ge(var_ready, m + 1)
                act.activation(rstd_of(m), rstd_of(m), ACT.Sqrt).then_inc(std_ready, 1)
                if nt is not None:
                    for k in range(KT):
                        act.wait_ge(nt_ready, m * KT + k + 1)
                        act.activation(xh[:, k, :], nt[:, k % 2, :], ACT.Copy).then_inc(nh_ready, 1)

            rstd_of = lambda m: (rstd1, rstd2, rstd3)[m][:, :]
            for k in range(KT):
                act.wait_ge(x_in[k // 4], 16)
                if k >= 2:
                    act.wait_ge(sq_used, k - 1)
                square(H1, sq1, k)
            for n in range(2):
                split_hi(act, n, n, first=True)
            norm_act(nt1)
            act.wait_ge(consts, 2)
            for n in range(N_LORA):
                act.wait_ge(w_used, n + 1)
                split_hi(act, n + 2, n % 2)
                if n:
                    act.wait_ge(lora_s, n)
                act.activation(plo[:, 1:T + 1], bank(6 + n % 2), ACT.Copy).then_inc(lora_p, 1)
                if n < 2:
                    act.wait_ge(lora_p, n + 1)
                    act.dma_start(if_d[n], plo[96:96 + MH, 1:T + 1]).then_inc(if_stored, 16)
                    act.wait_ge(if_stored, 16 * n + 16)
                act.wait_ge(lora_s, n + 1)
                f = (ACT.Tanh, ACT.Copy, ACT.Sigmoid, ACT.Sigmoid)[n]
                act.activation(lora[:, n, :], ysb[:, :], f).then_inc(lora_ready, 1)

            def act_a(j, c, first=False):
                n = tile_unit(j, c)
                act.wait_ge(w_used, n + 1)
                if not first:
                    act.wait_ge(shifted, 3 * j)
                act.activation(pin[c][:, 1:T + 1], bank(6 + c % 2), ACT.Copy).then_inc(pin_saved, 1)
                split_hi(act, n + 2, c % 2)

            def act_side(n, s, dst, saved, stored):
                act.wait_ge(w_used, n + 1)
                act.wait_ge(sg_stored[s], 16 * stored + 16)
                own(act, act.activation(sgb[:, s, :], bank(6 + s), ACT.Sigmoid), side_saved, saved)
                act.dma_start(dst.rearrange("a p t -> p (a t)"), sgb[:, s, :]).then_inc(sg_stored[s], 16)
                split_hi(act, n + 2, s)

            def act_o(j, saved, stored):
                act_side(tile_unit(j, 3), 1, og_d[bass.ds(j, 1)], saved, stored)

            def act_gate(j, c, n, last=0):
                stored = 2 * j + c // 2
                act_side(n, c % 2, sg_d[bass.ds(4 * j + c, 1)], 5 * j + 3 - last + c,
                         stored + j + 2 - last if c % 2 else stored)

            def act_prep(j, a):
                act.wait_ge(lw_mm, 3 * j + 3)
                act.activation(sg, bank(0), ACT.Sigmoid, bias=rp(j, 3))
                act.activation(a_, bank(1), ACT.Sigmoid, bias=rp(j, 4))
                act.activation(g_sb[:, :], bank(2), ACT.Copy).then_inc(lw_taken, 1)
                a(0)
                act.wait_ge(cs_ready, j + 1)
                act.activation(E1, cs, ACT.Exp, scale=-DECAY)
                act.activation(E2, cs, ACT.Exp, scale=DECAY)
                act.activation(E0, E0, ACT.Exp, scale=-DECAY).then_inc(exps_ready, 1)
                act.wait_ge(kksum_ready, j + 1)
                act.activation(t1, bank(3), ACT.Sqrt).then_inc(kknorm_ready, 1)
                a(1)

            def act_b(j, follow):
                follow(F_PREP)
                act.wait_ge(tr_ready, 4 * j + 2)
                act.activation(Vn[:, :, :].rearrange("p a b -> p (a b)"), bank(0), ACT.Copy).then_inc(tr_savedA, 1)
                act.activation(Bn[:, :, :].rearrange("p a b -> p (a b)"), bank(1), ACT.Copy).then_inc(tr_savedA, 1)
                follow(3 * F_INTRA + F_XT)
                for q in range(2):
                    act.wait_ge(x0_ready, 2 * j + q + 1)
                    act.activation(X[:, 4 * q:4 * q + 4, :], bank(q), ACT.Copy).then_inc(x0_saved, 1)
                follow(F_X0)
                for n in range(1, len(LEVELS)):
                    follow(F_Z)
                    if n < len(LEVELS) - 1:
                        for q in range(2):
                            act.wait_ge(xx_ready, 2 * (4 * j + n - 1) + q + 1)
                            act.activation(X[:, 4 * q:4 * q + 4, :], bank(2 + q), ACT.Copy).then_inc(x_saved, 1)
                    follow(F_X)
                act.wait_ge(wt_ready, j + 1)
                act.activation(WT[:, :], bank(0), ACT.Copy).then_inc(wt_saved, 1)
                follow(F_W)
                act.wait_ge(g_ready, j + 1)
                act.activation(Gn[:, :, :, :], ps[:, 2:4, :].rearrange("p b (n c) -> p b n c", n=TT)[:, :, :, 0:CH], ACT.Copy).then_inc(g_saved, 1)
                follow(F_G)
                for c in range(NCH):
                    follow(F_U)
                    follow(F_S)
                act.wait_ge(s_saved, NCH * j + NCH)
                act.wait_ge(y_ready, j + 1)
                act.activation(ysb[:, :], bank(0), ACT.Copy).then_inc(y_saved, 1)
                follow(F_YM + F_Y)
                act.wait_ge(yvar_ready, j + 1)
                act.activation(ysq[:, :], bank(5), ACT.Sqrt, scale=1.0 / CH, bias=cst[:, 0:1]).then_inc(ystd_ready, 1)
                act.wait_ge(yo_ready, j + 1)
                act.dma_start(yr_d[bass.ds(j, 1)].rearrange("a p t -> p (a t)"), ysb[:, :]).then_inc(yr_stored, 16)

            for s in range(2):
                act.sem_inc(sg_stored[s], 16)
            for c in range(3):
                act_a(0, c, first=True)
            act_o(0, 1, 0)
            with act.Fori(1, RJ) as i:
                def save(c):
                    if c == 0:
                        act_a(i, 2)
                    elif c == 1:
                        act_o(i, 5 * i - 3, 3 * i - 2)
                    else:
                        act_gate(i - 1, c - 2, tile_unit(i, c + 2))

                act_prep(i - 1, lambda c: act_a(i, c))
                act_b(i - 1, Follower(6, save))
                act.wait_ge(yr_stored, 16 * (i - 1) + 16)
            j = RJ - 1

            def save_last(c):
                if c < N_SIDE:
                    act_gate(j, c, U_MLSTM - N_SIDE + c, last=1)
                else:
                    act.wait_ge(w_used, U_MLSTM + c - N_SIDE + 1)
                    split_hi(act, U_MLSTM + c - N_SIDE + 2, c % 2)

            act_prep(j, save_last)
            act_b(j, Follower(N_SIDE, lambda c: save_last(c + 2)))
            act.wait_ge(yo_ready, RJ)

            def gate_rows():
                act.wait_ge(lf_e, 1)
                act.activation(rows[:, 3, :], rows[:, 2, :], ACT.Exp, scale=-1.0).then_inc(lf_ln, 1)
                act.wait_ge(lf_ln, 1)
                act.activation(rows[:, 4, :], rows[:, 3, :], ACT.Ln, bias=cst[0:MH, 1:2]).then_inc(lf_ln, 1)
                act.wait_ge(lf_e, 2)
                act.activation(rows[:, 4, :], rows[:, 6, :], ACT.Exp, scale=-1.0).then_inc(nm_ready, 1)

            def save_rows():
                for h in range(MH):
                    for c in range(2):
                        act.wait_ge(rb_ready, 2 * h + c + 1)
                        act.activation(RNb[:, h, c, :], bank(2 + c), ACT.Copy).then_inc(rb_saved, 1)

            def save_pc(h, c, first=False):
                n = U_MLSTM + 6 * h
                act.wait_ge(w_used, n + c + 1)
                if not first:
                    act.wait_ge(conv_ready, 4 * h + c - 3)
                act.activation(pc[c][:, 3:T + 3], bank(6 + c % 2), ACT.Copy).then_inc(pc_saved, 1)
                if not (first and c < 2):
                    split_hi(act, n + c + 2, c % 2)

            def silu(h, c):
                act.wait_ge(conv_ready, 4 * h + c + 1)
                act.activation(QK[:, c, :], cacc[:, c % 2, :], ACT.Silu).then_inc(qk_ready, 1)

            def save_v(h, first=False, between=None):
                n = U_MLSTM + 6 * h
                act.wait_ge(w_used, n + 5)
                split_hi(act, n + 6, 0)
                if between:
                    between()
                act.wait_ge(w_used, n + 6)
                if not first:
                    act.wait_ge(hm_ready, h)
                for c in range(2):
                    act.activation(Vm[:, 2 * c:2 * c + 2, :].rearrange("p a b -> p (a b)"), bank(c), ACT.Copy).then_inc(v_saved, 1)
                split_hi(act, n + 7, 1)

            def act_qk(h):
                act_att(h - 1)
                for c in range(4):
                    save_pc(h, c)
                    if c == 0:
                        act.wait_ge(sc_ready, TT * h)
                    silu(h, c)
                    if c == 2:
                        act_att_store(h - 1)

            def act_att(h):
                act.wait_ge(arg_ready, h + 1)
                for i in range(TT):
                    act.activation(Dm[:, i, P * i:T], Dm[:, i, P * i:T], ACT.Exp, scale=-1.0).then_inc(dm_ready, 1)

            def act_att_store(h):
                act.wait_ge(ym_ready, h + 1)
                act.dma_start(ym_d[bass.ds(2 * h, 2)].rearrange("a p t -> p a t"), ymo[:, :, :]).then_inc(ym_stored, 16)

            def load_og(h):
                act.dma_start(og[:, :, :], og_d[bass.ds(2 * h, 2)].rearrange("a p t -> p a t")).then_inc(og_in, 16)

            for c in range(2):
                save_pc(0, c, first=True)
            gate_rows()
            for c in range(2):
                silu(0, c)
            for c in range(2, 4):
                save_pc(0, c, first=True)
                silu(0, c)
            save_v(0, first=True)
            save_rows()
            with act.Fori(1, MH - 1) as h:
                load_og(h - 1)
                act_qk(h)
                save_v(h)
                act.wait_ge(ym_stored, 16 * h)

            def rwkv_hi(c):
                act.wait_ge(yr_in[c % 2], 16 * (c // 2) + 16)
                act.activation(yh_r[:, c, :], yrraw[c % 2][:, :], ACT.Copy).then_inc(yrh_ready, 1)

            load_og(MH - 2)
            act_qk(MH - 1)
            act.wait_ge(ym_stored, 16 * (MH - 1))
            load_og(MH - 1)
            act_att(MH - 1)
            for c in range(4):
                rwkv_hi(c)
            save_v(MH - 1, between=lambda: [rwkv_hi(c) for c in range(4, RJ)])

            act.wait_ge(ym_ready, MH)
            act.activation(yh_m[:, 2 * MH - 2:2 * MH, :], ymo[:, :, :], ACT.Copy).then_inc(ymh_ready, 1)
            for h in range(MH - 1):
                act.wait_ge(ym_in[h], 16)
                act.activation(yh_m[:, 2 * h:2 * h + 2, :], ymraw[:, h, :, :], ACT.Copy).then_inc(ymh_ready, 1)

            def act_mix(d, dd):
                split_hi(act, U_MIX + 2 * d + dd + 2, dd)
                act.wait_ge(mix_ready, 2 * d + dd + 1)
                act.activation(xh[:, bass.ds(2 * d + dd, 1), :].rearrange("p a t -> p (a t)"), mxo[:, dd, :], ACT.Copy).then_inc(mh_ready, 1)

            with act.Fori(0, KT // 2) as d:
                for dd in range(2):
                    act_mix(d, dd)
            act.wait_ge(w_used, U_OUT)
            act.wait_ge(ml_ready, KT)
            for c in range(4):
                act.dma_start(H[:, 4 * c:4 * c + 4, :], x_t[4 * c:4 * c + 4].rearrange("k p t -> p k t")).then_inc(h_in, 16)
            with act.Fori(0, KT // 2) as d:
                for c in range(2):
                    split_hi(act, U_OUT + 2 * d + c + 2, c)
            norm_act(nt2)
            act.dma_start(keys[:, :, :], keys_t).then_inc(keys_in, 16)

            def act_ahead(e, s, n):
                act.wait_ge(w_used, n + 1)
                act.wait_ge(pre_stored[s], 8 * e + 16 - 8 * s)
                own(act, act.activation(preb[:, s, :], bank(4 + s), ACT.Gelu), pre_ready, e + 1)
                act.dma_start(act_d[bass.ds(e, 1)].rearrange("a p t -> p (a t)"), preb[:, s, :]).then_inc(pre_stored[s], 16)
                split_hi(act, n + 2, s)

            def act_route(h, first=False):
                n = U_QUERY + 4 * h
                for c in range(2):
                    act.wait_ge(w_used, n + c + 1)
                    if not first:
                        act.wait_ge(key_scores, 2 * h + c - 1)
                    act.activation(qsb[:, c, :], bank(c), ACT.Copy).then_inc(q_saved, 1)
                    split_hi(act, n + c + 2, c)
                for c in range(2):
                    act.wait_ge(key_scores, 2 * h + c + 1)
                    if not first:
                        act.wait_ge(sel_done, 2 * h + c - 1)
                    act.activation(ssb[:, c, :, :].rearrange("p a b -> p (a b)"), bank(2 + c), ACT.Copy).then_inc(ssb_saved, 1)
                    act_ahead(2 * h + c, c, n + 2 + c)

            def act_softmax(h):
                act.wait_ge(best_ready, h + 1)
                act.activation(ex[:, :, :], ex[:, :, :], ACT.Exp).then_inc(ex_ready, 1)

            for s in range(2):
                act.sem_inc(pre_stored[s], 16)
            act_route(0, first=True)
            with act.Fori(1, HEADS) as h:
                act_route(h)
                act_softmax(h - 1)
            for e in range(N_TAIL):
                if e == N_TAIL - 1:
                    act_softmax(HEADS - 1)
                act_ahead(2 * HEADS + e, e % 2, U_TAIL + e)
            for m in range(3):
                act.wait_ge(egt_ready, m + 1)
                act.activation(EGT[:, m, :], bank(4 + m), ACT.Copy).then_inc(egt_saved, 1)
            def act_dense(b, s, first=False):
                if not first:
                    act.wait_ge(gates_stored[s], 8 * b - 8 * s)
                with act.Fori(0, GT // 16) as q:
                    for c in range(4):
                        act.wait_ge(oh_used, GT * b + 16 * q + 4 * c + 4)
                        act.activation(stage[s][:, :, bass.ds(16 * q + 4 * c, 4)].rearrange("p e t -> p t e"),
                                       bank(c).rearrange("p (t e) -> p t e", t=4), ACT.Copy).then_inc(dense_saved, 1)
                act.wait_ge(dense_saved, (GT // 4) * (b + 1))
                act.dma_start(gate_d[bass.ds(b, 1)].rearrange("a p e t -> p (a e t)"),
                              stage[s][:, :, :].rearrange("p e t -> p (e t)")).then_inc(gates_stored[s], 16)

            for s in range(2):
                act_dense(s, s, first=True)
            with act.Fori(1, GB // 2) as b:
                for s in range(2):
                    act_dense(2 * b + s, s)
            for s in range(2):
                act.wait_ge(gates_stored[s], 8 * GB)

            def load_group(g, s, ahead):
                for e in range(2):
                    act.dma_start(gt[:, s, e, :].rearrange("p (b t) -> p b t", b=GB),
                                  gate_d[:, :, bass.ds(2 * g + e, 1), :].rearrange("b p a t -> p b (a t)")).then_inc(gt_in[s], 16)
                if ahead:
                    act.dma_start(act_[:, s, :, :], act_d[bass.ds(2 * g, 2)].rearrange("a p t -> p a t")).then_inc(pre_in[s], 16)

            def act_halves(g, s):
                for e in range(2):
                    act.wait_ge(ga_ready, 2 * g + e + 1)
                    act.activation(gah[s][:, e, :], act_[:, s, e, :], ACT.Copy).then_inc(gah_ready, 1)

            def act_fetched(g, s, last=False):
                if not last:
                    act.wait_ge(gal_ready, 2 * g)
                    load_group(g + 1, 1 - s, True)
                act_halves(g, s)

            def act_scores(g, s, n0):
                act.wait_ge(gal_ready, 2 * g - 2)
                load_group(g, s, False)
                for e in range(2):
                    act.wait_ge(w_used, n0 + e + 1)
                    act.activation(act_[:, s, e, :], bank(e), ACT.Gelu).then_inc(gelu_ready, 1)
                    split_hi(act, n0 + e + 2, e)
                act_halves(g, s)

            def act_values(n0):
                for e in range(2):
                    act.wait_ge(w_used, n0 + e + 1)
                    split_hi(act, n0 + e + 2, e)

            for s in range(2):
                act.wait_ge(pre_stored[s], 16 + 8 * (2 * HEADS + N_TAIL))
                load_group(s, s, True)
            for e in range(N_TAIL, N_TAIL + 2):
                act_ahead(2 * HEADS + e, e % 2, U_TAIL + e)
            act_halves(0, 0)
            act_fetched(1, 1)
            act_values(U_PEER)
            for s in range(2):
                act.wait_ge(pre_stored[s], 16 + 16 * AHEAD)
            with act.Fori(1, AHEAD // 2 - 1) as i:
                for s in range(2):
                    act_fetched(2 * i + s, s)
                    act_values(U_PEER + 2 * (2 * i + s - 1))
            for s in range(2):
                act_fetched(AHEAD - 2 + s, s, last=s == 1)
                act_values(U_PEER + 2 * (AHEAD - 3 + s))
            with act.Fori(AHEAD // 2, GROUPS // 2) as i:
                for s in range(2):
                    g = 2 * i + s
                    act_scores(g, s, U_SCORED + 4 * (g - AHEAD))
                    act_values(U_SCORED + 4 * (g - AHEAD) + 2)
            for k in range(KT):
                act.wait_ge(out_added, KT * (GROUPS - 1) + k + 1)
                if k >= 2:
                    act.wait_ge(sq_summed, k - 1)
                square(H, sq3, k)
            norm_act(None)

        @block.vector
        def _(dve):
            step = Steps(dve, dve_step)
            st = {"norms": 0}
            rstd_of = lambda m: (rstd1, rstd2, rstd3)[m][:, :]

            def norm_dve(Hs, nt, gain):
                m = st["norms"]; st["norms"] += 1
                dve.wait_ge(var_sum, m + 1)
                dve.tensor_scalar(rstd_of(m), bank(7), 1.0 / D, RMS_EPS, ALU.mult, ALU.add).then_inc(var_ready, 1)
                dve.wait_ge(std_ready, m + 1)
                step(dve.reciprocal(rstd_of(m), rstd_of(m)))

                def normed(k):
                    if k >= 2:
                        dve.wait_ge(nl_ready, m * KT + k - 1)
                    dve.scalar_tensor_tensor(nt[:, k % 2, :], Hs[:, k, :], par[:, C_GAIN + m * KT + k:C_GAIN + m * KT + k + 1],
                                             rstd_of(m), ALU.mult, ALU.mult).then_inc(nt_ready, 1)
                normed(0)
                for k in range(KT):
                    if k + 1 < KT:
                        normed(k + 1)
                    dve.wait_ge(nh_ready, m * KT + k + 1)
                    dve.tensor_tensor(xl[:, k, :], nt[:, k % 2, :], xh[:, k, :].bitcast(F32), ALU.subtract).then_inc(nl_ready, 1)

            dve.wait_ge(par_in, 16)
            norm_dve(H1, nt1, 0)
            dve.wait_ge(consts, 2)

            def shift(dst, src, mu, signal, count):
                step(dve.tensor_tensor(t1, src[:, 0:T], src[:, 1:T + 1], ALU.subtract))
                own(dve, dve.scalar_tensor_tensor(dst, t1, mu, src[:, 1:T + 1], ALU.mult, ALU.add), signal, count)

            for n in range(N_LORA):
                dve.wait_ge(lora_p, n + 1)
                if n:
                    dve.wait_ge(lora_ready, n)
                shift(ysb[:, :], plo, par[:, C_LMU + n:C_LMU + n + 1], lora_s, n + 1)

            def dve_prep(j):
                dve.wait_ge(pin_saved, 3 * j + 3)
                for c, dst in enumerate((r_, k_, v_)):
                    shift(dst, pin[c], rp(j, c), shifted, 3 * j + c + 1)
                step(dve.tensor_scalar(kk, k_, rp(j, 5), None, ALU.mult))
                own(dve, dve.tensor_tensor(t2, kk, kk, ALU.mult), kk_ready, j + 1)
                dve.wait_ge(lw_taken, j + 1)
                step(dve.tensor_tensor_scan(cs, reset[:, :], sg, 0.0, ALU.mult, ALU.add))
                own(dve, dve.tensor_tensor(E0, cs, sg, ALU.subtract), cs_ready, j + 1)
                step(dve.tensor_scalar(sg, a_, 1.0, rp(j, 6), ALU.subtract, ALU.mult))
                step(dve.scalar_tensor_tensor(k_, sg, 1.0, k_, ALU.add, ALU.mult))
                dve.wait_ge(kksum_ready, j + 1)
                own(dve, dve.scalar_tensor_tensor(t2, r_, rp(j, 7), k_, ALU.mult, ALU.mult), bprod_ready, j + 1)
                dve.wait_ge(exps_ready, j + 1)
                step(dve.tensor_tensor(AR[:, 1, :], r_, E1, ALU.mult))
                step(dve.tensor_tensor(Kt[:, :], k_, E2, ALU.mult))
                step(dve.tensor_copy(EL[:, :], E1.rearrange("p (c u) -> p c u", u=CH)[:, :, CH - 1]))
                dve.wait_ge(kknorm_ready, j + 1)
                step(dve.tensor_scalar(t1, t1, L2_EPS, None, ALU.max))
                step(dve.reciprocal(sg, t1))
                step(dve.tensor_tensor(kk, kk, sg, ALU.mult))
                step(dve.scalar_tensor_tensor(AR[:, 0, :], kk, -1.0, E0, ALU.mult, ALU.mult))
                step(dve.tensor_tensor(kk, kk, a_, ALU.mult))
                step(dve.tensor_tensor(Bt[:, :], kk, E2, ALU.mult))
                dve.wait_ge(bsum_ready, j + 1)
                dve.tensor_tensor(bonus[:, :], bank(4), v_, ALU.mult).then_inc(prep_done, 1)
                dve.wait_ge(prep_done, j + 1)

            idb = ident[:, :].unsqueeze(1).to_broadcast([P, 8, P])

            def level_mask(n):
                return lev[:, n, :].unsqueeze(1).to_broadcast([P, 8, P])

            def dve_b(j):
                dve.wait_ge(tr_ready, 4 * j + 4)
                dve.tensor_copy(Kn[:, :, :].rearrange("p a b -> p (a b)"), bank(2)).then_inc(tr_savedD, 1)
                dve.tensor_copy(An[:, :, :].rearrange("p a b -> p (a b)"), bank(3)).then_inc(tr_savedD, 1)
                for m in range(8):
                    dve.wait_ge(intra_ready, 8 * j + m + 1)
                    dve.tensor_tensor(M4[:, m, :, :], bank(4 + m % 2).rearrange("p (a t) -> p a t", a=4), mask4[:, :, :],
                                      ALU.mult).then_inc(intra_saved, 1)
                dve.wait_ge(intra_saved, 8 * j + 8)
                step(dve.tensor_tensor(XT[:, :, :], M4[:, :, 0, :], level_mask(0), ALU.mult))
                dve.tensor_tensor(XT[:, :, :], XT[:, :, :], idb, ALU.add).then_inc(xt0_ready, 1)
                own(dve, dve.tensor_tensor(Mb[:, :, :], M4[:, :, 0, :], level_mask(1), ALU.mult), mb_ready, 5 * j + 1)
                for n in range(1, len(LEVELS)):
                    m = 5 * j + n - 1
                    for q in range(2):
                        dve.wait_ge(z_ready, 2 * m + q + 1)
                        dve.tensor_tensor(Z[:, 4 * q:4 * q + 4, :], bank(q).rearrange("p (a t) -> p a t", a=4), idb[:, 0:4, :],
                                          ALU.add).then_inc(z_saved, 1)
                    if n + 1 < len(LEVELS):
                        dve.tensor_tensor(Mb[:, :, :], M4[:, :, 0, :], level_mask(n + 1), ALU.mult).then_inc(mb_ready, 1)
                    for q in range(2):
                        dve.wait_ge(xt_ready, 2 * m + q + 1)
                        dve.tensor_copy(XT[:, 4 * q:4 * q + 4, :], bank(4 + q).rearrange("p (a t) -> p a t", a=4)).then_inc(xt_saved, 1)
                dve.wait_ge(akv_ready, j + 1)
                v = ps[:, 4:6, :].rearrange("p b (n h c) -> p b n h c", n=TT, h=2)
                for h in range(2):
                    last = dve.tensor_copy(AKV[:, h, :, :], v[:, h, :, h, :])
                    last.then_inc(akv_saved, 1)
                dve.wait_ge(g_saved, j + 1)
                for c in range(NCH):
                    tt, q = divmod(c, 2)
                    rows_ = slice(CH * q, CH * q + CH)
                    dve.wait_ge(u_ready, NCH * j + c + 1)
                    dve.tensor_tensor(Un[rows_, tt, :, :], bank(3)[rows_, 0:P].rearrange("p (h c) -> p h c", h=2),
                                      Gn[rows_, :, tt, :], ALU.add).then_inc(u_saved, 1)
                    step(dve.tensor_scalar(SE[:, :], Sh[:, c, :], EL[:, c:c + 1], None, ALU.mult))
                    dve.wait_ge(s_ready, NCH * j + c + 1)
                    step(dve.scalar_tensor_tensor(Sh[0:CH, c + 1, 0:CH], bank(4)[0:CH, 0:CH], EL[0:CH, c:c + 1], SE[0:CH, 0:CH],
                                                  ALU.mult, ALU.add))
                    own(dve, dve.scalar_tensor_tensor(Sh[CH:P, c + 1, CH:P], bank(4)[CH:P, CH:P], EL[CH:P, c:c + 1], SE[CH:P, CH:P],
                                                      ALU.mult, ALU.add), s_saved, NCH * j + c + 1)
                dve.wait_ge(y_saved, j + 1)
                dve.wait_ge(mean_ready, j + 1)
                step(dve.scalar_tensor_tensor(yc[:, :], bank(1), -1.0 / CH, ysb[:, :], ALU.mult, ALU.add))
                own(dve, dve.tensor_tensor(ysq[:, :], yc[:, :], yc[:, :], ALU.mult), ysq_ready, j + 1)
                dve.wait_ge(ystd_ready, j + 1)
                step(dve.reciprocal(ysb[:, :], ysq[:, :]))
                step(dve.tensor_tensor(yc[:, :], yc[:, :], ysb[:, :], ALU.mult))
                step(dve.tensor_scalar(yc[:, :], yc[:, :], rp(j, 8), rp(j, 9), ALU.mult, ALU.add))
                step(dve.tensor_tensor(yc[:, :], yc[:, :], bonus[:, :], ALU.add))

            def dve_y(j):
                own(dve, dve.tensor_tensor(ysb[:, :], yc[:, :], g_sb[:, :], ALU.mult), yo_ready, j + 1)

            with dve.Fori(0, RJ) as j:
                step.enter(j, 0, STEPS_RWKV)
                dve_prep(j)
                dve_b(j)
                dve_y(j)
                step.leave(RJ)

            dve.wait_ge(consts, 3)
            dve.wait_ge(rows_in, 32)
            row = lambda n: rows[:, n, :]
            step(dve.tensor_scalar(row(0), row(0), par[0:MH, C_BI:C_BI + 1], None, ALU.add))
            step(dve.tensor_scalar(row(1), row(1), par[0:MH, C_BI + 1:C_BI + 2], None, ALU.add))
            own(dve, dve.scalar_tensor_tensor(row(2), row(1), -1.0, row(1), ALU.mult, ALU.max), lf_e, 1)
            step(dve.tensor_scalar(row(1), row(1), 0.0, None, ALU.min))
            dve.wait_ge(lf_ln, 2)
            step(dve.tensor_tensor(row(1), row(1), row(4), ALU.subtract))
            step(dve.tensor_tensor_scan(row(2), row(7), row(1), 0.0, ALU.mult, ALU.add))
            dve.tensor_tensor(row(3), row(0), row(2), ALU.subtract).then_inc(rows_ready, 1)
            dve.wait_ge(rows_ready, 1)
            step(dve.tensor_tensor_scan(row(5), row(7), row(3), 0.0, ALU.mult, ALU.max))
            dve.tensor_tensor(row(6), row(2), row(5), ALU.add).then_inc(lf_e, 1)
            dve.wait_ge(lf_e, 2)
            def conv(h, c, first=False):
                t = [h * 2, h * 2 + 1, 8 + h * 2, 8 + h * 2 + 1][c]
                w = lambda u: par[:, bass.ds(C_CONV + 4 * t + u, 1)]
                dve.wait_ge(pc_saved, 4 * h + c + 1)
                if c >= 2:
                    dve.wait_ge(qk_ready, 4 * h + c - 1)
                elif not first:
                    dve.wait_ge(qk_ready, 4 * h + c - 1)
                a = cacc[:, c % 2, :]
                step(dve.tensor_scalar(a, pc[c][:, 0:T], w(0), None, ALU.mult))
                for u in range(1, 3):
                    step(dve.scalar_tensor_tensor(a, pc[c][:, u:u + T], w(u), a, ALU.mult, ALU.add))
                dve.scalar_tensor_tensor(a, pc[c][:, 3:T + 3], w(3), a, ALU.mult, ALU.add).then_inc(conv_ready, 1)
                dve.wait_ge(conv_ready, 4 * h + c + 1)

            def dve_args(h):
                for i in range(TT):
                    last = dve.tensor_scalar(Dm[:, i, P * i:T], RNb[:, bass.ds(h, 1), 0, P * i:T].rearrange("p a t -> p (a t)"),
                                             rcol[:, i, bass.ds(h, 1)], 0.0, ALU.subtract, ALU.max)
                last.then_inc(arg_ready, 1)

            SC = [(2, 0), (3, 0), (4, 0), (3, 384)]

            def dve_weights(h):
                dve.wait_ge(sc_ready, TT * h + TT)
                dve.wait_ge(dm_ready, TT * h + TT)
                for i in range(TT):
                    lo = P * i
                    b, at = SC[i]
                    step(dve.scalar_tensor_tensor(SD[:, i, lo:T], bank(b)[:, at:at + T - lo], 1.0 / 16.0, Dm[:, i, lo:T],
                                                  ALU.mult, ALU.mult))
                    dve.tensor_tensor(SD[:, i, lo:lo + P], SD[:, i, lo:lo + P], tri[:, :], ALU.mult).then_inc(sd_ready, 1)

            def dve_heads(h):
                dve.wait_ge(den_ready, h + 1)
                step(dve.scalar_tensor_tensor(rec[:, :], bank(3), -1.0, RNb[:, bass.ds(h, 1), 1, :].rearrange("p a t -> p (a t)"),
                                              ALU.mult, ALU.max))
                step(dve.tensor_tensor(rec[:, :], bank(3), rec[:, :], ALU.max))
                step(dve.reciprocal(rec[:, :], rec[:, :]))
                dve.wait_ge(hm_ready, h + 1)
                dve.wait_ge(og_in, 16 * h + 16)
                for c in range(2):
                    step(dve.tensor_tensor(ymo[:, c, :], bank((5, 2)[c]), rec[:, :], ALU.mult))
                own(dve, dve.tensor_tensor(ymo[:, :, :], ymo[:, :, :], og[:, :, :], ALU.mult), ym_ready, h + 1)

            for c in range(4):
                conv(0, c, first=True)
            dve.wait_ge(rc_ready, 1)
            own(dve, dve.tensor_copy(rcol[:, :, :].rearrange("p a b -> p (a b)"), bank(4)[:, 0:TT * MH]), rc_saved, 1)
            dve.wait_ge(rb_saved, 2 * MH)
            with dve.Fori(1, MH) as h:
                step.enter(h, 1, STEPS_MLSTM)
                dve_args(h - 1)
                conv(h, 0)
                dve_weights(h - 1)
                conv(h, 1)
                dve_heads(h - 1)
                conv(h, 2)
                conv(h, 3)
                step.leave(MH - 1)
            dve_args(MH - 1)
            dve_weights(MH - 1)
            dve_heads(MH - 1)

            at = slice(2 * MH - 2, 2 * MH)
            dve.wait_ge(ymh_ready, 1)
            dve.tensor_tensor(yl_m[:, at, :], ymo[:, :, :], yh_m[:, at, :].bitcast(F32), ALU.subtract).then_inc(yml_ready, 1)
            for h in range(MH - 1):
                at = slice(2 * h, 2 * h + 2)
                dve.wait_ge(ymh_ready, h + 2)
                dve.tensor_tensor(yl_m[:, at, :], ymraw[:, h, :, :], yh_m[:, at, :].bitcast(F32), ALU.subtract).then_inc(yml_ready, 1)
            dve.wait_ge(yml_ready, MH)

            def merge(d, dd):
                k = 2 * d + dd
                dve.wait_ge(sg_in[dd], 32 * d + 32)
                dve.wait_ge(w_used, U_MIX + k + 1)
                for c in range(2):
                    step(dve.tensor_tensor(sgm[:, dd, c, :], bank(dd + 6 * c), sgm[:, dd, c, :], ALU.mult))
                own(dve, dve.tensor_tensor(mxo[:, dd, :], sgm[:, dd, 0, :], sgm[:, dd, 1, :], ALU.add), mix_ready, k + 1)
                dve.wait_ge(mh_ready, k + 1)
                at = lambda t: t[:, bass.ds(k, 1), :].rearrange("p a t -> p (a t)")
                own(dve, dve.tensor_tensor(at(xl), mxo[:, dd, :], at(xh).bitcast(F32), ALU.subtract), ml_ready, k + 1)

            with dve.Fori(0, KT // 2) as d:
                step.enter(d, 0, 4)
                for dd in range(2):
                    merge(d, dd)
                step.leave(KT // 2)
            dve.wait_ge(h_in, 64)
            step(dve.memset(sum2[:, :], 0.0))
            with dve.Fori(0, KT // 2) as d:
                step.enter(d, 0, 4)
                for c in range(2):
                    dve.wait_ge(w_used, U_OUT + 2 * d + c + 1)
                    hk = H[:, bass.ds(2 * d + c, 1), :].rearrange("p a t -> p (a t)")
                    own(dve, dve.tensor_tensor(hk, bank(c), hk, ALU.add), h_ready, 2 * d + c + 1)
                    step(dve.tensor_tensor(sq2[:, :], hk, hk, ALU.mult))
                    step(dve.tensor_tensor(sum2[:, :], sum2[:, :], sq2[:, :], ALU.add))
                step.leave(KT // 2)
            dve.sem_inc(sum_ready, 1)
            norm_dve(H, nt2, 1)

            def top16(vals, idx, src, rep):
                dve.sem_inc(passed, 1)
                step(dve.max(vals[:, 0:8], src))
                dve.sem_inc(passed, 1)
                step(dve.max_index(idx[:, 0:8], vals[:, 0:8], src))
                dve.sem_inc(passed, 1)
                step(dve.match_replace(rep, vals[:, 0:8], src, -3.0e38))
                dve.sem_inc(passed, 1)
                step(dve.max(vals[:, 8:16], rep))
                dve.sem_inc(passed, 1)
                step(dve.max_index(idx[:, 8:16], vals[:, 8:16], rep))

            with dve.Fori(0, HEADS) as h:
                step.enter(h, 0, STEPS_ROUTE)
                for c in range(2):
                    dve.wait_ge(ssb_saved, 2 * h + c + 1)
                    for tt in range(TT):
                        top16(v16[:, c, tt, :], i16[:, c, tt, :], ssb[:, c, tt, :], srep[:, :])
                    dve.tensor_copy(if16[:, c, :, :], i16[:, c, :, :]).then_inc(sel_done, 1)
                dve.wait_ge(sel_done, 2 * h + 2)
                for tt in range(TT):
                    c3 = lambda t: t[:, :].rearrange("p (a b) -> p a b", a=TOPK)
                    step(dve.tensor_tensor(c3(cand), v16[:, 0, tt, :].unsqueeze(2).to_broadcast([P, TOPK, TOPK]),
                                           v16[:, 1, tt, :].unsqueeze(1).to_broadcast([P, TOPK, TOPK]), ALU.add))
                    top16(best[:, tt, :], ci[:, tt, :], cand[:, :], crep[:, :])
                dve.tensor_tensor(ex[:, :, :], best[:, :, :], best[:, :, 0:1].to_broadcast([P, TT, TOPK]), ALU.subtract).then_inc(best_ready, 1)
                step(dve.tensor_scalar(chi[:, 0, :, :], ci[:, :, :], 4, None, ALU.logical_shift_right))
                step(dve.tensor_scalar(chi[:, 1, :, :], ci[:, :, :], 15, None, ALU.bitwise_and))
                step(dve.tensor_copy(chf[:, :, :, :], chi[:, :, :, :]))
                for tt in range(TT):
                    for c in range(2):
                        step(dve.tensor_tensor(eq[:, :, :], chf[:, c, tt, :].unsqueeze(2).to_broadcast([P, TOPK, TOPK]),
                                               iota16[:, :].unsqueeze(1).to_broadcast([P, TOPK, TOPK]), ALU.is_equal))
                        step(dve.tensor_tensor(eq[:, :, :], eq[:, :, :], if16[:, c, tt, :].unsqueeze(1).to_broadcast([P, TOPK, TOPK]), ALU.mult))
                        step(dve.tensor_reduce(EG[:, c, tt, bass.ds(TOPK * h, TOPK)], eq[:, :, :], AX.X, ALU.add))
                dve.wait_ge(ex_ready, h + 1)
                step(dve.tensor_reduce(sm[:, 0, :], ex[:, :, :], AX.X, ALU.add))
                step(dve.reciprocal(sm[:, 1, :], sm[:, 0, :]))
                dve.tensor_tensor(EG[:, 2, :, bass.ds(TOPK * h, TOPK)], ex[:, :, :], sm[:, 1, :].unsqueeze(2).to_broadcast([P, TT, TOPK]),
                                  ALU.mult).then_inc(routed, 1)
                dve.wait_ge(routed, h + 1)
                step.leave(HEADS)
            dve.wait_ge(egt_saved, 3)

            def onehots(i, first=False):
                for c in range(OH // 4):
                    if not first:
                        dve.wait_ge(oh_used, OH * i + 4 * c + 4 - OH)
                    for m, rows_of in ((1, oh2), (0, oh1)):
                        last = dve.tensor_tensor(rows_of[:, 4 * c:4 * c + 4, :], iota128[:, :].unsqueeze(1).to_broadcast([P, 4, P]),
                                                 EGT[:, m, bass.ds(OH * i + 4 * c, 4)].unsqueeze(2).to_broadcast([P, 4, P]),
                                                 ALU.is_equal)
                    last.then_inc(oh_ready, 1)

            onehots(0, first=True)
            with dve.Fori(1, T // OH) as i:
                onehots(i)

            def dve_gated(g, s, ahead):
                dve.wait_ge(gt_in[s], 16 * (g - s) + 32)
                if ahead:
                    dve.wait_ge(pre_in[s], 8 * (g - s) + 16)
                for e in range(2):
                    if not ahead:
                        dve.wait_ge(gelu_ready, 2 * (g - AHEAD) + e + 1)
                    dve.tensor_tensor(act_[:, s, e, :], act_[:, s, e, :], gt[:, s, e, :], ALU.mult).then_inc(ga_ready, 1)
                for e in range(2):
                    dve.wait_ge(gah_ready, 2 * g + e + 1)
                    dve.tensor_tensor(gal[s][:, e, :], act_[:, s, e, :], gah[s][:, e, :].bitcast(F32), ALU.subtract).then_inc(gal_ready, 1)

            def dve_values(g, n0, behind=None):
                for d in range(KT):
                    if d % 8 == 7:
                        dve.wait_ge(w_used, n0 + d // 8 + 1)
                    else:
                        dve.wait_ge(out_ready, 14 * g + d - d // 8 + 1)
                    dve.tensor_tensor(H[:, d, :], bank(2 + d % 4), H[:, d, :], ALU.add).then_inc(out_added, 1)
                    if behind and d:
                        behind(d - 1)
                if behind:
                    behind(KT - 1)

            dve_gated(0, 0, True)
            dve_gated(1, 1, True)
            dve_values(0, U_PEER)
            with dve.Fori(1, AHEAD // 2) as i:
                for s in range(2):
                    g = 2 * i + s
                    dve_gated(g, s, True)
                    dve_values(g - 1, U_PEER + 2 * (g - 1))
            with dve.Fori(AHEAD // 2, GROUPS // 2) as i:
                for s in range(2):
                    g = 2 * i + s
                    dve_gated(g, s, False)
                    dve_values(g - 1, U_SCORED + 4 * (g - AHEAD) + 2)
            def add_square(k):
                dve.wait_ge(sq_ready, KT + k + 1)
                own(dve, dve.tensor_tensor(sum3[:, :], sum3[:, :], sq3[:, k % 2, :], ALU.add), sq_summed, k + 1)

            step(dve.memset(sum3[:, :], 0.0))
            dve_values(GROUPS - 1, N_UNITS - 2, add_square)
            dve.sem_inc(sum_ready, 1)
            m = st["norms"]
            dve.wait_ge(var_sum, m + 1)
            dve.tensor_scalar(rstd_of(m), bank(7), 1.0 / D, RMS_EPS, ALU.mult, ALU.add).then_inc(var_ready, 1)
            dve.wait_ge(std_ready, m + 1)
            step(dve.reciprocal(rstd_of(m), rstd_of(m)))
            for k in range(KT):
                c = C_GAIN + m * KT + k
                dve.scalar_tensor_tensor(H[:, k, :], H[:, k, :], par[:, c:c + 1], rstd_of(m), ALU.mult, ALU.mult).then_inc(last_ready, 1)

        @block.tensor
        def _(pe):
            st = {"norms": 0}

            def norm_pe(m, total):
                pe.wait_ge(sum_ready, m)
                pe.matmul(bank(7), ones[:, :], total[:, :], start=True, stop=True).then_inc(var_sum, 1)

            def first_units(n, dst, m):
                for s in range(2):
                    pe.wait_ge(w_lo, n + s + 1)
                for k in range(KT):
                    pe.wait_ge(nl_ready, m * KT + k + 1)
                    for s in range(2):
                        last = products(pe, bank(dst + s), s, k, P, xh, xl, k, k == 0, k == KT - 1)
                        if k == KT - 1:
                            last.then_inc(w_used, 1)

            pe.wait_ge(consts, 1)
            for k in range(KT):
                pe.wait_ge(sq_ready, k + 1)
                last = pe.matmul(bank(7), ones[:, :], sq1[:, k % 2, :], start=k == 0, stop=k == KT - 1)
                last.then_inc(sq_used, 1) if k < KT - 1 else last.then_inc(var_sum, 1)
            first_units(0, 6, 0)
            for n in range(2, N_LORA):
                pe.wait_ge(lora_p, n - 1)
                unit(pe, n, n % 2, bank(6 + n % 2))

            def unit_waits(i, c):
                if isinstance(i, int) and i == 0:
                    pe.wait_ge(lora_p, 3 + c) if c < 2 else pe.wait_ge(pin_saved, c - 1)
                elif c < 2:
                    pe.wait_ge(side_saved, 5 * i - 4)
                elif c < 5:
                    pe.wait_ge(pin_saved, 3 * i + c - 1)
                else:
                    pe.wait_ge(side_saved, 5 * i - 8 + c)

            def pe_prep(j, n, waits):
                pe.wait_ge(lw_in, 16 * j + 16)
                pe.wait_ge(lora_ready, N_LORA)
                pe.matmul(bank(0), lw[:, 0, :], lora[:, 0, :], start=True, stop=True).then_inc(lw_mm, 1)
                pe.matmul(bank(1), lw[:, 1, :], lora[:, 1, :], start=True, stop=True).then_inc(lw_mm, 1)
                pe.matmul(bank(2), lw[:, 2, :], lora[:, 2, :], start=True, stop=False)
                pe.matmul(bank(2), lw[:, 3, :], lora[:, 3, :], start=False, stop=True).then_inc(lw_mm, 1)
                waits(0)
                unit(pe, n, 0, bank(6))
                waits(1)
                unit(pe, n + 1, 1, bank(7), 0, 7)
                pe.wait_ge(kk_ready, j + 1)
                pe.matmul(bank(3), headones[:, :], t2, start=True, stop=True).then_inc(kksum_ready, 1)
                unit(pe, n + 1, 1, bank(7), 7, 12)
                pe.wait_ge(bprod_ready, j + 1)
                pe.matmul(bank(4), headones[:, :], t2, start=True, stop=True).then_inc(bsum_ready, 1)
                unit(pe, n + 1, 1, bank(7), 12, KT)

            def pe_b(j, fill):
                fill(F_PREP)
                pe.wait_ge(prep_done, j + 1)
                for n, (src, dst) in enumerate(((v_, 0), (Bt[:, :], 1), (Kt[:, :], 2), (AR[:, 0, :], 3))):
                    for tt in range(TT):
                        last = pe.transpose(bank(dst)[:, tt * P:tt * P + P], src[:, tt * P:tt * P + P], ident[:, :])
                    last.then_inc(tr_ready, 1)
                hs = [slice(CH * h, CH * h + CH) for h in range(2)]
                for m in range(8):
                    h, tt = divmod(m, TT)
                    t = slice(P * tt, P * tt + P)
                    if m >= 2:
                        pe.wait_ge(intra_saved, 8 * j + m - 1)
                    for n, lhs in enumerate((Bt, Kt)):
                        last = pe.matmul(bank(4 + m % 2)[:, 256 * n:256 * n + 256].rearrange("p (a t) -> p a t", a=2),
                                         lhs[hs[h], t], AR[hs[h], :, t], start=True, stop=True)
                    last.then_inc(intra_ready, 1)
                    if m % 2 and m < 7:
                        fill(F_INTRA)
                fill(F_XT)
                pe.wait_ge(xt0_ready, j + 1)
                pe.wait_ge(tr_savedA, 2 * j + 2)
                for m in range(8):
                    last = pe.transpose(bank(m // 4)[:, (m % 4) * P:(m % 4) * P + P], XT[:, m, :], ident[:, :])
                    if m % 4 == 3:
                        last.then_inc(x0_ready, 1)
                fill(F_X0)
                pe.wait_ge(tr_savedD, 2 * j + 2)
                pe.wait_ge(intra_saved, 8 * j + 8)
                part = lambda b, m: bank(b + m // 4)[:, (m % 4) * P:(m % 4) * P + P]
                for n in range(1, len(LEVELS)):
                    lv = 5 * j + n - 1
                    pe.wait_ge(mb_ready, lv + 1)
                    if n == 1:
                        pe.wait_ge(x0_saved, 2 * j + 2)
                    else:
                        pe.wait_ge(x_saved, 2 * (4 * j + n - 1))
                    for m in range(8):
                        last = pe.matmul(part(0, m), Mb[:, m, :], X[:, m, :], start=True, stop=True)
                        if m % 4 == 3:
                            last.then_inc(z_ready, 1)
                    fill(F_Z)
                    pe.wait_ge(z_saved, 2 * lv + 2)
                    if n > 1:
                        pe.wait_ge(xt_saved, 2 * lv)
                    if n < len(LEVELS) - 1:
                        for m in range(8):
                            last = pe.matmul(part(2, m), XT[:, m, :], Z[:, m, :], start=True, stop=True)
                            if m % 4 == 3:
                                last.then_inc(xx_ready, 1)
                    for m in range(8):
                        last = pe.matmul(part(4, m), Z[:, m, :], XT[:, m, :], start=True, stop=True)
                        if m % 4 == 3:
                            last.then_inc(xt_ready, 1)
                    fill(F_X)
                pe.wait_ge(xt_saved, 2 * (5 * j + 5))
                for m in range(8):
                    h, tt = divmod(m, TT)
                    last = pe.matmul(bank(0)[hs[h], P * tt:P * tt + P], An[:, tt, hs[h]], XT[:, m, :], start=True, stop=True)
                last.then_inc(wt_ready, 1)
                for m in range(8):
                    h, tt = divmod(m, TT)
                    last = pe.matmul(part(4, m), M4[:, m, 2, :], Vn[:, tt, :], start=True, stop=True)
                last.then_inc(akv_ready, 1)
                fill(F_W)
                pe.wait_ge(akv_saved, 2 * j + 2)
                for m in range(8):
                    h, tt = divmod(m, TT)
                    last = pe.matmul(part(2, m), XT[:, m, :], AKVf[:, CH * m:CH * m + P], start=True, stop=True)
                last.then_inc(g_ready, 1)
                fill(F_G)
                pe.wait_ge(wt_saved, j + 1)
                pe.wait_ge(g_saved, j + 1)
                for c in range(NCH):
                    tt, q = divmod(c, 2)
                    pe.matmul(bank(3)[hs[q], 0:P], WT[:, CH * c:CH * c + CH], Sh[:, c, :], start=True, stop=True).then_inc(u_ready, 1)
                    fill(F_U)
                    pe.wait_ge(u_saved, NCH * j + c + 1)
                    pe.matmul(bank(4)[:, 0:P], Kn[hs[q], tt, :], Vn[hs[q], tt, :], start=True, stop=False)
                    pe.matmul(bank(4)[:, 0:P], Bn[hs[q], tt, :], Un[hs[q], tt, :, :].rearrange("p h c -> p (h c)"),
                              start=False, stop=True).then_inc(s_ready, 1)
                    fill(F_S)
                    pe.wait_ge(s_saved, NCH * j + c + 1)
                for c in range(NCH):
                    pe.matmul(bank(0)[:, CH * c:CH * c + CH], Sh[:, c, :], AR[:, 1, CH * c:CH * c + CH],
                              start=c == 0, stop=False, skip_group_check=True)
                for h in range(2):
                    for tt in range(TT):
                        dst = bank(0)[hs[h], P * tt:P * tt + P]
                        pe.matmul(dst, Un[:, tt, h, :], M4[:, TT * h + tt, 1, :], start=False, stop=False, skip_group_check=True)
                        last = pe.matmul(dst, Vn[:, tt, hs[h]], M4[:, TT * h + tt, 3, :], start=False, stop=True, skip_group_check=True)
                last.then_inc(y_ready, 1)
                fill(F_YM)
                pe.wait_ge(y_saved, j + 1)
                pe.matmul(bank(1), headones[:, :], ysb[:, :], start=True, stop=True).then_inc(mean_ready, 1)
                fill(F_Y)
                pe.wait_ge(ysq_ready, j + 1)
                pe.matmul(bank(5), headones[:, :], ysq[:, :], start=True, stop=True).then_inc(yvar_ready, 1)

            for c in range(4):
                unit_waits(0, c)
                unit(pe, tile_unit(0, c), c % 2, bank(6 + c % 2))
            pe.wait_ge(consts, 2)
            with pe.Fori(1, RJ) as i:
                pe_prep(i - 1, tile_unit(i, 0), lambda c: unit_waits(i, c))
                pe_b(i - 1, Filler(pe, tile_unit(i, 2), 6, lambda c: unit_waits(i, 2 + c)))
            last_waits = lambda c: pe.wait_ge(side_saved, 5 * RJ - 4 + max(c - 1, 0))
            pe_prep(RJ - 1, U_MLSTM - N_SIDE, last_waits)
            pe_b(RJ - 1, Filler(pe, U_MLSTM - 2, N_SIDE, lambda c: last_waits(c + 2)))

            def pe_gate_rows():
                pe.wait_ge(rows_ready, 1)
                for tt in range(TT):
                    last = pe.transpose(bank(4)[:, MH * tt:MH * tt + MH], rows[:, 3, tt * P:tt * P + P], ident[0:MH, 0:MH])
                last.then_inc(rc_ready, 1)
                pe.wait_ge(nm_ready, 1)
                for h in range(MH):
                    for c, src in enumerate((5, 4)):
                        if h:
                            pe.wait_ge(rb_saved, 2 * h + c - 1)
                        pe.matmul(bank(2 + c), sel[:, h, :], rows[:, src, :], start=True, stop=True).then_inc(rb_ready, 1)

            def pe_qk(h, c):
                pe.wait_ge(pc_saved, 4 * h + c - 1 if c >= 2 else 4 * h)
                unit(pe, U_MLSTM + 6 * h + c, c % 2, bank(6 + c % 2))

            def pe_v(h, first=False):
                n = U_MLSTM + 6 * h
                if not first:
                    pe.wait_ge(v_saved, 2 * h)
                for c in range(2):
                    pe.wait_ge(w_lo, n + 5 + c)
                    for tt in range(TT):
                        dst = bank(tt // 2)[:, 256 * (tt % 2):256 * (tt % 2) + 256]
                        for k in range(8):
                            lh, ll = xh[:, 8 * c + k, P * tt:P * tt + P], xl[:, 8 * c + k, P * tt:P * tt + P]
                            w_h, w_l = wh[c][:, 256 * k:256 * k + 256], wl[c][:, 256 * k:256 * k + 256]
                            new = c == 0 and k == 0 and tt % 2 == 0
                            pe.matmul(dst, lh, w_h, start=new, stop=False, skip_group_check=True)
                            pe.matmul(dst, lh, w_l, start=False, stop=False, skip_group_check=True)
                            last = pe.matmul(dst, ll, w_h, start=False, stop=c == 1 and k == 7, skip_group_check=True)
                    last.then_inc(w_used, 1)

            SC = [(2, 0), (3, 0), (4, 0), (3, 384)]

            def pe_scores_m(h):
                pe.wait_ge(qk_ready, 4 * h + 4)
                for i in range(TT):
                    lo = P * i
                    b, at = SC[i]
                    for c in range(2):
                        last = pe.matmul(bank(b)[:, at:at + T - lo], QK[:, 2 + c, lo:lo + P], QK[:, c, lo:T], start=c == 0, stop=c == 1)
                    last.then_inc(sc_ready, 1)

            def pe_heads(h):
                pe.wait_ge(v_saved, 2 * h + 2)
                pe.wait_ge(sd_ready, TT * h + TT)
                for b, lhs, ready in ((3, lambda i: ones[:, :], den_ready), (5, lambda i: Vm[:, i, 0:P], None),
                                      (2, lambda i: Vm[:, i, P:2 * P], hm_ready)):
                    for i in range(TT):
                        last = pe.matmul(bank(b)[:, P * i:T], lhs(i), SD[:, i, P * i:T], start=i == 0, stop=i == TT - 1)
                    if ready:
                        last.then_inc(ready, 1)

            for c in range(2, 4):
                pe_qk(0, c)
            pe_v(0, first=True)
            pe_gate_rows()
            pe.wait_ge(rb_saved, 2 * MH)
            pe.wait_ge(rc_saved, 1)
            with pe.Fori(1, MH) as h:
                pe_qk(h, 0)
                pe_scores_m(h - 1)
                pe_qk(h, 1)
                pe_heads(h - 1)
                for c in range(2, 4):
                    pe_qk(h, c)
                pe_v(h)
            pe_scores_m(MH - 1)
            pe_heads(MH - 1)

            def pe_mix_r(d, dd):
                pe.wait_ge(w_lo, U_MIX + 2 * d + dd + 1)
                for k in range(8):
                    products(pe, bank(6 + dd), dd, 8 + k, P, yh_r, yl_r, k, k == 0, k == 7)

            def pe_mix_m(d, dd, first=False):
                for n, k in enumerate((6, 7, 0, 1, 2, 3, 4, 5)):
                    if first and n % 2 == 0:
                        pe.wait_ge(yml_ready, n // 2 + 1)
                    last = products(pe, bank(dd), dd, k, P, yh_m, yl_m, k, n == 0, n == 7)
                last.then_inc(w_used, 1)

            pe.wait_ge(yrl_ready, RJ)
            pe.wait_ge(pc_saved, 4 * MH)
            for dd in range(2):
                pe_mix_r(0, dd)
            for dd in range(2):
                pe_mix_m(0, dd, first=dd == 0)
            with pe.Fori(1, KT // 2) as d:
                for dd in range(2):
                    pe.wait_ge(mix_ready, 2 * d + dd - 1)
                    pe_mix_r(d, dd)
                    pe_mix_m(d, dd)
            pe.wait_ge(mix_ready, KT)
            for c in range(2):
                pe.wait_ge(w_lo, U_OUT + c + 1)
                for k in range(KT):
                    pe.wait_ge(ml_ready, k + 1)
                    last = products(pe, bank(c), c, k, P, xh, xl, k, k == 0, k == KT - 1)
                last.then_inc(w_used, 1)
            with pe.Fori(1, KT // 2) as d:
                for c in range(2):
                    pe.wait_ge(h_ready, 2 * d + c - 1)
                    unit(pe, U_OUT + 2 * d + c, c, bank(c))
            norm_pe(1, sum2)

            def key_products(h, c):
                pe.wait_ge(q_saved, 2 * h + c + 1)
                for tt in range(TT):
                    last = pe.matmul(bank(2 + c)[:, P * tt:P * tt + P], qsb[:, c, P * tt:P * tt + P], keys[:, c, :], start=True, stop=True)
                last.then_inc(key_scores, 1)

            first_units(U_QUERY, 0, 1)
            pe.wait_ge(keys_in, 16)

            def ahead(e, s, n):
                if not (isinstance(e, int) and e < 2):
                    pe.wait_ge(pre_ready, e - 1)
                unit(pe, n, s, bank(4 + s))

            for c in range(2):
                key_products(0, c)
                ahead(c, c, U_QUERY + 2 + c)
            with pe.Fori(1, HEADS) as h:
                for c in range(2):
                    unit(pe, U_QUERY + 4 * h + c, c, bank(c))
                for c in range(2):
                    pe.wait_ge(ssb_saved, 2 * h + c - 1)
                    key_products(h, c)
                    ahead(2 * h + c, c, U_QUERY + 4 * h + 2 + c)
            for e in range(N_TAIL):
                ahead(2 * HEADS + e, e % 2, U_TAIL + e)
            pe.wait_ge(routed, HEADS)
            pe.wait_ge(pre_ready, 2 * HEADS + N_TAIL)
            for m in range(3):
                for tt in range(TT):
                    last = pe.transpose(bank(4 + m)[:, P * tt:P * tt + P], EG[:, m, tt, :], ident[:, :])
                last.then_inc(egt_ready, 1)

            def dense(i, first=False):
                for c in range(4):
                    if not first:
                        pe.wait_ge(dense_saved, 4 * i + c - 3)
                    pe.wait_ge(gated_ready, 4 * i + c + 1)
                    for u in range(4):
                        last = pe.matmul(bank(c)[:, P * u:P * u + P], oh2[:, 4 * c + u, :], oh1[:, 4 * c + u, :], start=True, stop=True)
                        last.then_inc(oh_used, 1)

            dense(0, first=True)
            with pe.Fori(1, T // 16) as i:
                dense(i)

            def pe_scores(g, n0, first=False):
                for e in range(2):
                    if not first:
                        pe.wait_ge(gelu_ready, 2 * (g - AHEAD) + e - 1)
                    unit(pe, n0 + e, e, bank(e))

            def pe_values(g, s, n0, first=False):
                pe.wait_ge(gal_ready, 2 * g + 2)
                for half in range(2):
                    pe.wait_ge(w_lo, n0 + half + 1)
                    for dd in range(8):
                        d = 8 * half + dd
                        if not (first and d < 4):
                            pe.wait_ge(out_added, KT * g + d - 3)
                        for e in range(2):
                            last = products(pe, bank(2 + d % 4), half, 8 * e + dd, P, gah[s], gal[s], e, e == 0, e == 1)
                        if dd == 7:
                            last.then_inc(w_used, 1)
                        else:
                            last.then_inc(out_ready, 1)

            pe.wait_ge(egt_saved, 3)
            for e in range(N_TAIL, N_TAIL + 2):
                ahead(2 * HEADS + e, e % 2, U_TAIL + e)
            pe.wait_ge(dense_saved, T // 4)
            pe.wait_ge(pre_ready, 2 * AHEAD)
            pe_values(0, 0, U_PEER, first=True)
            with pe.Fori(1, AHEAD // 2) as i:
                for s in range(2):
                    g = 2 * i + s
                    pe_values(g - 1, (s + 1) % 2, U_PEER + 2 * (g - 1))
            for s in range(2):
                pe_scores(AHEAD + s, U_SCORED + 4 * s, first=s == 0)
                pe_values(AHEAD + s - 1, (s + 1) % 2, U_SCORED + 4 * s + 2)
            with pe.Fori(AHEAD // 2 + 1, GROUPS // 2) as i:
                for s in range(2):
                    g = 2 * i + s
                    pe_scores(g, U_SCORED + 4 * (g - AHEAD))
                    pe_values(g - 1, (s + 1) % 2, U_SCORED + 4 * (g - AHEAD) + 2)
            pe_values(GROUPS - 1, 1, N_UNITS - 2)
            norm_pe(2, sum3)


STEPS_RWKV, STEPS_MLSTM, STEPS_ROUTE = 38, 21, 93


_INS = ["stream", "lora_w", "params", "x_t", "keys_t"]


def layout(i):
    import numpy as np
    a = {k: np.asarray(v) for k, v in i.items()}
    w_in = a["w_in"][0]
    stream = np.zeros((N_UNITS, P, 2048), np.float32)
    tile = lambda w: w.reshape(-1, P, P).transpose(1, 0, 2).reshape(P, -1)
    RB = 4 * 1024 + 2 * MH
    GBASE = RB + 3 * 1024 + 96 + 96 + 256
    pad = np.zeros((D, 28), np.float32)
    for n in range(2):
        low = w_in[:, RB + 3072 + 96 * n:RB + 3072 + 96 * n + 96]
        stream[n] = tile(np.concatenate([low, w_in[:, 4096 + MH * n:4096 + MH * n + MH], pad], 1))
        stream[2 + n] = tile(w_in[:, RB + 3264 + P * n:RB + 3264 + P * n + P])
    for j in range(RJ):
        at = U_RWKV + max(8 * j - 4, 0)
        for c in range(3):
            stream[at + c] = tile(w_in[:, RB + 1024 * c + P * j:RB + 1024 * c + P * j + P])
        stream[at + 3] = tile(w_in[:, 3072 + P * j:3072 + P * j + P])
        for c in range(N_SIDE):
            q = N_SIDE * j + c
            stream[min(U_RWKV + 8 * (j + 1), U_MLSTM - N_SIDE) + c] = tile(w_in[:, GBASE + P * q:GBASE + P * q + P])
    for h in range(MH):
        for c in range(4):
            at = 1024 * (c // 2) + 256 * h + P * (c % 2)
            stream[U_MLSTM + 6 * h + c] = tile(w_in[:, at:at + P])
        for c in range(2):
            v = w_in[1024 * c:1024 * c + 1024, 2048 + 256 * h:2048 + 256 * h + 256]
            stream[U_MLSTM + 6 * h + 4 + c] = v.reshape(8, P, 256).transpose(1, 0, 2).reshape(P, 2048)
    for d in range(KT):
        cut = slice(P * d, P * d + P)
        stream[U_MIX + d] = tile(np.concatenate([a["proj_mlstm"][0][:, cut], a["proj_rwkv"][0][:, cut]], 0))
        stream[U_OUT + d] = tile(a["w_out"][0][:, cut])
        stream[U_QUERY + 4 * (d // 2) + d % 2] = tile(a["peer_w_query"][0][:, cut])
    u = a["peer_u"][0].reshape(NKEYS, NKEYS, KT, P).transpose(0, 3, 2, 1).reshape(NKEYS, P, 2048)
    v = a["peer_v"][0].reshape(GROUPS, 2, NKEYS, 2, 1024).transpose(0, 3, 2, 1, 4).reshape(GROUPS, 2, P, 2048)
    for g in range(GROUPS):
        at = U_QUERY + 4 * g + 2 if g < HEADS else U_TAIL + 2 * (g - HEADS) if g < AHEAD else U_SCORED + 4 * (g - AHEAD)
        stream[at:at + 2] = u[2 * g:2 * g + 2]
        at = U_PEER + 2 * g if g < AHEAD - 1 else U_SCORED + 4 * (g - AHEAD + 1) + 2 if g < GROUPS - 1 else N_UNITS - 2
        stream[at:at + 2] = v[g]
    lora = np.zeros((4, P, 1024), np.float32)
    lora[0, :96], lora[1, :96] = a["rwkv_w2"][0], a["rwkv_a2"][0]
    lora[2:4] = a["rwkv_g2"][0].reshape(2, P, 1024)
    lora_w = np.ascontiguousarray(lora.reshape(4, P, RJ, P).transpose(2, 1, 0, 3))
    par = np.zeros((P, N_PAR), np.float32)
    mu = a["rwkv_mu"][0]
    per = [mu[0:1024], mu[1024:2048], mu[2048:3072], a["rwkv_w0"][0], a["rwkv_a0"][0], a["rwkv_k_k"][0],
           a["rwkv_k_a"][0], a["rwkv_r_k"][0].reshape(-1), a["rwkv_ln_w"][0], a["rwkv_ln_b"][0]]
    par[:, 0:C_LMU] = np.stack(per).reshape(N_RP, RJ, P).transpose(2, 1, 0).reshape(P, -1)
    par[:96, C_LMU], par[:96, C_LMU + 1] = mu[3072:3168], mu[3168:3264]
    par[:, C_LMU + 2:C_LMU + 4] = mu[3264:3520].reshape(2, P).T
    par[:MH, C_BI], par[:MH, C_BI + 1] = a["mlstm_b_i"][0], a["mlstm_b_f"][0]
    par[:, C_CONV:C_GAIN] = a["mlstm_conv"][0].reshape(4, 16, P).transpose(2, 1, 0).reshape(P, -1)
    gains = np.stack([a["norm_mix_gain"][0], a["norm_ffn_gain"][0], a["norm_final_gain"]])
    par[:, C_GAIN:] = gains.reshape(3, KT, P).transpose(2, 0, 1).reshape(P, -1)
    x_t = np.ascontiguousarray(a["x"][0].T.reshape(KT, P, T))
    keys_t = np.ascontiguousarray(a["peer_sub_keys"][0].transpose(2, 0, 1))
    return {"stream": stream, "lora_w": lora_w, "params": par, "x_t": x_t, "keys_t": keys_t}


def kernel(**inputs):
    import numpy as np
    import concourse.bacc as bacc
    from concourse.bass_utils import run_bass_kernel_spmd

    nc = bacc.Bacc("TRN2", target_bir_lowering=False, num_devices=1)
    arrays = layout(inputs)
    args = [nc.dram_tensor(k, arrays[k].shape, F32, kind="ExternalInput").ap() for k in _INS]
    out = nc.dram_tensor("out", (KT, P, T), F32, kind="ExternalOutput").ap()
    build(nc, *args, out)
    r = run_bass_kernel_spmd(nc, [arrays], core_ids=[0])
    y = r.results[0]["out"]
    return np.ascontiguousarray(y.reshape(D, T).T).reshape(1, T, D)
```
